# Optimizing a Trainium2 kernel written in Bass

```python
import jax, jax.numpy as jnp
from jax import lax
import numpy as np

D_MODEL = 2048
BATCH = 1
SEQ = 256
DEPTH = 2

N_META = 16
NORM_EPS = 1e-6
LRU_WIDTH = D_MODEL // 2
LRU_BLOCKS = 16
LRU_BLOCK = LRU_WIDTH // LRU_BLOCKS
LRU_CONV = 4
LRU_C = 8.0
RWKV_HEADS = 16
RWKV_HEAD_DIM = 64
RWKV_WIDTH = RWKV_HEADS * RWKV_HEAD_DIM
RWKV_W_RANK = 64
RWKV_A_RANK = 64
RWKV_G_RANK = 128
RWKV_GN_EPS = 64e-5
RWKV_IN = 3 * RWKV_WIDTH + RWKV_W_RANK + RWKV_A_RANK + RWKV_G_RANK
AB_IN = 2 * LRU_WIDTH + RWKV_IN
AB_MIX = LRU_WIDTH + RWKV_WIDTH
GLA_HEADS = 4
GLA_DK = D_MODEL // 2 // GLA_HEADS
GLA_DV = D_MODEL // GLA_HEADS
GLA_KW = GLA_HEADS * GLA_DK
GLA_VW = GLA_HEADS * GLA_DV
GLA_GATE_RANK = 16
GLA_GATE_NORM = 16.0
GLA_CHUNK = 64
GLA_IN = 2 * GLA_KW + 2 * GLA_VW + GLA_GATE_RANK
D_FF = 5632
FFN_CONV = 3
N_EVEN = (DEPTH + 1) // 2
N_ODD = DEPTH // 2

kernel_name = 'hybrid_rglru_rwkv7_gla_convffn'

def rmsnorm(x, w):
    xf = x.astype(jnp.float32)
    y = xf * lax.rsqrt(jnp.mean(xf * xf, -1, keepdims=True) + NORM_EPS)
    return (y * w.astype(jnp.float32)).astype(x.dtype)

def causal_dwconv(x, w, b):
    K, C = w.shape
    y = lax.conv_general_dilated(x, w[:, None, :].astype(x.dtype), window_strides=(1,),
                                 padding=[(K - 1, 0)], dimension_numbers=('NWC', 'WIO', 'NWC'),
                                 feature_group_count=C)
    return y + b.astype(x.dtype)

def token_shift(x):
    return jnp.pad(x, ((0, 0), (1, 0), (0, 0)))[:, :-1]

def rglru(xc, ga_w, ga_b, gx_w, gx_b, lam):
    B, T, _ = xc.shape
    xf = xc.astype(jnp.float32)
    xb = xf.reshape(B, T, LRU_BLOCKS, LRU_BLOCK)
    r = jax.nn.sigmoid(jnp.einsum('bthi,hij->bthj', xb, ga_w).reshape(B, T, LRU_WIDTH) + ga_b)
    i = jax.nn.sigmoid(jnp.einsum('bthi,hij->bthj', xb, gx_w).reshape(B, T, LRU_WIDTH) + gx_b)
    log_a = -LRU_C * r * jax.nn.softplus(-lam)
    a = jnp.exp(log_a)
    u = jnp.sqrt(-jnp.expm1(2.0 * log_a)) * (i * xf)

    def combine(left, right):
        a1, b1 = left
        a2, b2 = right
        return a1 * a2, a2 * b1 + b2

    _, h = lax.associative_scan(combine, (a, u), axis=1)
    return h.astype(xc.dtype)

def rwkv7(u_in, shift_mu, w0, w2, a0, a2, g2, k_k, k_a, r_k, ln_w, ln_b):
    B, T, _ = u_in.shape
    u = u_in.astype(jnp.float32)
    u = u + (token_shift(u) - u) * shift_mu
    o1 = RWKV_WIDTH
    o2 = 2 * RWKV_WIDTH
    o3 = 3 * RWKV_WIDTH
    o4 = o3 + RWKV_W_RANK
    o5 = o4 + RWKV_A_RANK
    r, k, v, wd, ad, gd = jnp.split(u, [o1, o2, o3, o4, o5], axis=-1)
    w = -jax.nn.softplus(-(w0 + jnp.tanh(wd) @ w2)) - 0.5
    decay = jnp.exp(-jnp.exp(w))
    a = jax.nn.sigmoid(a0 + ad @ a2)
    g = jax.nn.sigmoid(gd) @ g2
    heads = lambda t: t.reshape(B, T, RWKV_HEADS, RWKV_HEAD_DIM)
    kk = heads(k * k_k)
    kk = kk / jnp.maximum(jnp.sqrt(jnp.sum(kk * kk, -1, keepdims=True)), 1e-12)
    k = k * (1.0 + (a - 1.0) * k_a)
    rh, kh, vh, dh, ah = heads(r), heads(k), heads(v), heads(decay), heads(a)

    def step(S, inp):
        r_t, w_t, k_t, v_t, kk_t, a_t = inp
        s_kk = jnp.einsum('bhvk,bhk->bhv', S, kk_t)
        S = (S * w_t[:, :, None, :] - s_kk[..., None] * (kk_t * a_t)[:, :, None, :]
             + v_t[..., None] * k_t[:, :, None, :])
        return S, jnp.einsum('bhvk,bhk->bhv', S, r_t)

    xs = tuple(jnp.moveaxis(t, 1, 0) for t in (rh, dh, kh, vh, kk, ah))
    S0 = jnp.zeros((B, RWKV_HEADS, RWKV_HEAD_DIM, RWKV_HEAD_DIM), jnp.float32)
    _, y = lax.scan(step, S0, xs)
    y = jnp.moveaxis(y, 0, 1)
    mu = jnp.mean(y, -1, keepdims=True)
    var = jnp.mean(jnp.square(y - mu), -1, keepdims=True)
    y = ((y - mu) * lax.rsqrt(var + RWKV_GN_EPS)).reshape(B, T, RWKV_WIDTH) * ln_w + ln_b
    bonus = (jnp.sum(rh * kh * r_k, -1, keepdims=True) * vh).reshape(B, T, RWKV_WIDTH)
    return ((y + bonus) * g).astype(u_in.dtype)

def hybrid_ab(h, w_in, lru_conv_w, lru_conv_b, ga_w, ga_b, gx_w, gx_b, lam,
              shift_mu, w0, w2, a0, a2, g2, k_k, k_a, r_k, ln_w, ln_b, w_out):
    u = h @ w_in
    lx = u[..., :LRU_WIDTH]
    ly = u[..., LRU_WIDTH:2 * LRU_WIDTH]
    ur = u[..., 2 * LRU_WIDTH:]
    lx = causal_dwconv(lx, lru_conv_w, lru_conv_b)
    lru_out = rglru(lx, ga_w, ga_b, gx_w, gx_b, lam) * jax.nn.gelu(ly)
    rw_out = rwkv7(ur, shift_mu, w0, w2, a0, a2, g2, k_k, k_a, r_k, ln_w, ln_b)
    return jnp.concatenate([lru_out, rw_out], -1) @ w_out

def gla_mixer(h, w_in, gk_up, gk_b, norm_w, w_out):
    B, T, _ = h.shape
    u = (h @ w_in).astype(jnp.float32)
    q, k, v, g, gd = jnp.split(u, [GLA_KW, 2 * GLA_KW, 2 * GLA_KW + GLA_VW, 2 * GLA_KW + 2 * GLA_VW], axis=-1)
    gk = jax.nn.log_sigmoid(gd @ gk_up + gk_b) / GLA_GATE_NORM
    q = q * (GLA_DK ** -0.5)
    pad = (-N_META) % GLA_CHUNK
    L = T + pad
    NC = L // GLA_CHUNK

    def to_chunks(t, d):
        t = jnp.pad(t.reshape(B, T, GLA_HEADS, d), ((0, 0), (pad, 0), (0, 0), (0, 0)))
        return t.reshape(B, NC, GLA_CHUNK, GLA_HEADS, d).transpose(1, 0, 3, 2, 4)

    qc, kc, gc = to_chunks(q, GLA_DK), to_chunks(k, GLA_DK), to_chunks(gk, GLA_DK)
    vc = to_chunks(v, GLA_DV)
    mask = jnp.tril(jnp.ones((GLA_CHUNK, GLA_CHUNK), bool))

    def step(S, inp):
        q_c, k_c, v_c, g_c = inp
        b = jnp.cumsum(g_c, axis=2)
        o_inter = jnp.einsum('bhcd,bhde->bhce', q_c * jnp.exp(b), S)
        diff = b[:, :, :, None, :] - b[:, :, None, :, :]
        dec = jnp.exp(jnp.where(mask[:, :, None], diff, -jnp.inf))
        A = jnp.sum(q_c[:, :, :, None, :] * k_c[:, :, None, :, :] * dec, -1)
        o = o_inter + jnp.einsum('bhij,bhje->bhie', A, v_c)
        b_last = b[:, :, -1:, :]
        S = S * jnp.exp(b_last[:, :, 0, :])[..., None] + jnp.einsum('bhcd,bhce->bhde', k_c * jnp.exp(b_last - b), v_c)
        return S, o

    S0 = jnp.zeros((B, GLA_HEADS, GLA_DK, GLA_DV), jnp.float32)
    _, o = lax.scan(step, S0, (qc, kc, vc, gc))
    o = o.transpose(1, 0, 3, 2, 4).reshape(B, L, GLA_HEADS, GLA_DV)[:, pad:]
    o = rmsnorm(o, norm_w).reshape(B, T, GLA_VW) * jax.nn.silu(g)
    return o.astype(h.dtype) @ w_out

def conv_ffn(h, w_gate, w_val, conv_w, conv_b, w_down):
    gate = causal_dwconv(h @ w_gate, conv_w, conv_b)
    return (jax.nn.gelu(gate) * (h @ w_val)) @ w_down

def setup_inputs(seed: int = 0) -> dict:
    key = jax.random.key(seed)
    ks = iter(jax.random.split(key, 48))
    f32 = jnp.float32

    def nrm(shape, scale):
        return jax.random.normal(next(ks), shape, f32) * scale

    def gain(shape):
        return 1.0 + 0.02 * jax.random.normal(next(ks), shape, f32)

    s = jax.random.uniform(next(ks), (N_EVEN, LRU_WIDTH), f32, 0.9, 0.999) ** (1.0 / LRU_C)
    return {
        'x': nrm((BATCH, SEQ, D_MODEL), 1.0),
        'meta_tokens': nrm((N_META, D_MODEL), 1.0),
        'mix_pre_norm': gain((DEPTH, D_MODEL)),
        'mix_post_norm': gain((DEPTH, D_MODEL)),
        'ffn_pre_norm': gain((DEPTH, D_MODEL)),
        'ffn_post_norm': gain((DEPTH, D_MODEL)),
        'ab_w_in': nrm((N_EVEN, D_MODEL, AB_IN), D_MODEL ** -0.5),
        'lru_conv_w': nrm((N_EVEN, LRU_CONV, LRU_WIDTH), LRU_CONV ** -0.5),
        'lru_conv_b': nrm((N_EVEN, LRU_WIDTH), 0.02),
        'lru_gate_a_w': nrm((N_EVEN, LRU_BLOCKS, LRU_BLOCK, LRU_BLOCK), LRU_BLOCK ** -0.5),
        'lru_gate_a_b': nrm((N_EVEN, LRU_WIDTH), 0.02),
        'lru_gate_x_w': nrm((N_EVEN, LRU_BLOCKS, LRU_BLOCK, LRU_BLOCK), LRU_BLOCK ** -0.5),
        'lru_gate_x_b': nrm((N_EVEN, LRU_WIDTH), 0.02),
        'lru_lambda': jnp.log(s) - jnp.log1p(-s),
        'rwkv_shift_mu': jax.random.uniform(next(ks), (N_EVEN, RWKV_IN), f32),
        'rwkv_w0': jax.random.uniform(next(ks), (N_EVEN, RWKV_WIDTH), f32, -6.0, 1.0),
        'rwkv_w2': nrm((N_EVEN, RWKV_W_RANK, RWKV_WIDTH), 0.5 * RWKV_W_RANK ** -0.5),
        'rwkv_a0': nrm((N_EVEN, RWKV_WIDTH), 0.1),
        'rwkv_a2': nrm((N_EVEN, RWKV_A_RANK, RWKV_WIDTH), 0.5 * RWKV_A_RANK ** -0.5),
        'rwkv_g2': nrm((N_EVEN, RWKV_G_RANK, RWKV_WIDTH), RWKV_G_RANK ** -0.5),
        'rwkv_k_k': 0.85 + nrm((N_EVEN, RWKV_WIDTH), 0.05),
        'rwkv_k_a': gain((N_EVEN, RWKV_WIDTH)),
        'rwkv_r_k': nrm((N_EVEN, RWKV_HEADS, RWKV_HEAD_DIM), 0.1),
        'rwkv_ln_w': gain((N_EVEN, RWKV_WIDTH)),
        'rwkv_ln_b': nrm((N_EVEN, RWKV_WIDTH), 0.02),
        'ab_w_out': nrm((N_EVEN, AB_MIX, D_MODEL), AB_MIX ** -0.5),
        'gla_w_in': nrm((N_ODD, D_MODEL, GLA_IN), D_MODEL ** -0.5),
        'gla_gk_up': nrm((N_ODD, GLA_GATE_RANK, GLA_KW), GLA_GATE_RANK ** -0.5),
        'gla_gk_b': nrm((N_ODD, GLA_KW), 0.1),
        'gla_norm_w': gain((N_ODD, GLA_DV)),
        'gla_w_out': nrm((N_ODD, GLA_VW, D_MODEL), GLA_VW ** -0.5),
        'ffn_w_gate': nrm((DEPTH, D_MODEL, D_FF), D_MODEL ** -0.5),
        'ffn_w_val': nrm((DEPTH, D_MODEL, D_FF), D_MODEL ** -0.5),
        'ffn_conv_w': nrm((DEPTH, FFN_CONV, D_FF), FFN_CONV ** -0.5),
        'ffn_conv_b': nrm((DEPTH, D_FF), 0.02),
        'ffn_w_down': nrm((DEPTH, D_FF, D_MODEL), D_FF ** -0.5),
    }

def reference(x, meta_tokens, mix_pre_norm, mix_post_norm, ffn_pre_norm, ffn_post_norm,
              ab_w_in, lru_conv_w, lru_conv_b, lru_gate_a_w, lru_gate_a_b, lru_gate_x_w, lru_gate_x_b,
              lru_lambda, rwkv_shift_mu, rwkv_w0, rwkv_w2, rwkv_a0, rwkv_a2, rwkv_g2, rwkv_k_k, rwkv_k_a,
              rwkv_r_k, rwkv_ln_w, rwkv_ln_b, ab_w_out, gla_w_in, gla_gk_up, gla_gk_b, gla_norm_w,
              gla_w_out, ffn_w_gate, ffn_w_val, ffn_conv_w, ffn_conv_b, ffn_w_down):
    B = x.shape[0]
    meta = jnp.broadcast_to(meta_tokens[None].astype(x.dtype), (B, N_META, D_MODEL))
    h = jnp.concatenate([meta, x], axis=1)
    for layer in range(DEPTH):
        j = layer // 2
        hn = rmsnorm(h, mix_pre_norm[layer])
        if layer % 2 == 0:
            m = hybrid_ab(hn, ab_w_in[j], lru_conv_w[j], lru_conv_b[j], lru_gate_a_w[j], lru_gate_a_b[j],
                          lru_gate_x_w[j], lru_gate_x_b[j], lru_lambda[j], rwkv_shift_mu[j], rwkv_w0[j],
                          rwkv_w2[j], rwkv_a0[j], rwkv_a2[j], rwkv_g2[j], rwkv_k_k[j], rwkv_k_a[j],
                          rwkv_r_k[j], rwkv_ln_w[j], rwkv_ln_b[j], ab_w_out[j])
        else:
            m = gla_mixer(hn, gla_w_in[j], gla_gk_up[j], gla_gk_b[j], gla_norm_w[j], gla_w_out[j])
        h = h + rmsnorm(m, mix_post_norm[layer])
        f = conv_ffn(rmsnorm(h, ffn_pre_norm[layer]), ffn_w_gate[layer], ffn_w_val[layer],
                     ffn_conv_w[layer], ffn_conv_b[layer], ffn_w_down[layer])
        h = h + rmsnorm(f, ffn_post_norm[layer])
    return h[:, N_META:]


_drawn_inputs = setup_inputs


def setup_inputs(seed=0):
    import zlib

    import numpy as np

    out = dict(_drawn_inputs(seed))
    spreads = {}
    factors = {'ffn_post_norm': 2.895,
     'lru_gate_a_b': 43.251,
     'lru_gate_x_b': 27.324,
     'rwkv_k_a': 2.714,
     'rwkv_ln_w': 2.935,
     'rwkv_ln_b': 2.716,
     'gla_norm_w': 40.653,
     'ffn_conv_b': 2.945,
     'gla_gk_b': 3.475}
    for name, (base, spread) in spreads.items():
        noise = np.random.default_rng([zlib.crc32(name.encode()), seed]).standard_normal(out[name].shape)
        drawn = base * np.exp(spread * noise) if base else spread * noise
        out[name] = __import__('jax').numpy.asarray(drawn.astype(out[name].dtype))
    for name, factor in factors.items():
        out[name] = (out[name] * factor).astype(out[name].dtype)
    return out
```

```python
import concourse.bass as bass
from concourse import mybir
from contextlib import ExitStack, contextmanager
import numpy as np

F32 = mybir.dt.float32
F32R = mybir.dt.float32r
ALU = mybir.AluOpType
ACT = mybir.ActivationFunctionType
ds = bass.ds

P = 128
D_MODEL = 2048
KT = D_MODEL // P
N_META = 16
SEQ = 256
T = N_META + SEQ
D_FF = 5632
PANEL = 256
UNIT_KT = 4
UNITS = 4
RAW_SLOTS = 8
SPLIT_SLOTS = 4
LRU_WIDTH = 1024
RW = 1024
GLA_KW = 1024
GLA_VW = 2048
FFN_PARTS = ((0, 8), (8, 8), (16, 6))
NORM_EPS = 1e-6
GN_EPS = 64e-5
DECAY = float(np.exp(-0.5))
CH = 64
LEVELS = (2, 4, 8, 16, 32)
TAIL = T - 2 * P
GLA_LEVELS = (1, 2, 4, 8, 16, 32, 64)
GLA_DK = 256
GLA_DV = 512

PARAM_ROWS = [("mix_pre", 32), ("mix_post", 32), ("ffn_pre", 32), ("ffn_post", 32),
              ("lru_cw", 32), ("lru_cb", 8), ("ga_b", 8), ("gx_b", 8), ("lam", 8),
              ("mu", 26), ("w0", 8), ("a0", 8), ("k_k", 8), ("k_a", 8), ("r_k", 8), ("ln_w", 8), ("ln_b", 8),
              ("gk_b", 8), ("gla_nw", 4), ("ffn_cw", 264), ("ffn_cb", 88)]
COL, _c = {}, 0
for _n, _r in PARAM_ROWS:
    COL[_n] = _c
    _c += _r
N_COLS = _c
PT_GROUPS = -(-N_COLS // P)
DCOL = {"one_minus_mu": 0, "one_minus_ka": 26, "neg8sp": 34, "pos8sp": 42}
N_DCOLS = 50


def constants():
    t = np.arange(P)
    row, col = t[:, None], t[None, :]
    same = (row // CH) == (col // CH)
    strict_up, incl_up = (row < col) & same, (row <= col) & same
    parts = [strict_up, incl_up, strict_up, -1.0 * incl_up, (row > col) & same]
    pair_low = (row // 2 == col // 2) & (row > col)
    parts += [pair_low, pair_low.T]
    for size in LEVELS:
        parts.append((row // (2 * size) == col // (2 * size)) & (row // size > col // size))
    chunk = np.stack([t // CH == 0, t // CH == 1], 1)
    restart = np.ones((P, T))
    restart[:, ::CH] = 0.0
    parts += [chunk, -1.0 * chunk, restart]
    rwkv = np.concatenate([np.asarray(p, np.float32) for p in parts], 1)
    scale = GLA_DK ** -0.5
    gla = [scale * (row == col)]
    for size in GLA_LEVELS:
        gla.append(scale * ((row // (2 * size) == col // (2 * size)) & (row // size < col // size)))
    gla = np.concatenate([np.asarray(p, np.float32) for p in gla], 1)
    head = (row // 64) == (col // 64)
    trunk = np.concatenate([np.asarray(p, np.float32) for p in (row == col, np.ones((P, P)), head)], 1)
    return rwkv, gla, trunk


def phases(upto):
    out = [("wag", 1, [("ab_w_in", 2 * LRU_WIDTH + 3 * RW, 0, 0, 4)]),
           ("rkv", 6, [("ab_w_in", 2 * LRU_WIDTH + PANEL * k, 2 * PANEL, 0, 4) for k in range(2)]),
           ("lru", 4, [("ab_w_in", 0, PANEL, 0, 4), ("ab_w_in", LRU_WIDTH, PANEL, 0, 4)]),
           ("out0", 4, [("ab_w_out", PANEL * k, 2 * PANEL, 0, 4) for k in range(2)])]

    def ffn(layer):
        for n, (first, count) in enumerate(FFN_PARTS):
            out.append((f"gv{layer}_{n}", count, [(f"{w}{layer}", PANEL * first, PANEL, 0, 4) for w in ("gate", "val")]))
            out.append((f"dn{layer}_{n}", 4, [(f"down{layer}", PANEL * k, 2 * PANEL, PANEL * first, count // 2)
                                              for k in range(2)]))
    if upto >= 2:
        ffn(0)
    if upto >= 3:
        qkv = 2 * GLA_KW + GLA_VW
        out.append(("gla_qkv", 8, [("gla_w_in", PANEL * k, 2 * PANEL, 0, 4) for k in range(2)]))
        out.append(("gla_g", 4, [("gla_w_in", qkv + PANEL * k, 2 * PANEL, 0, 4) for k in range(2)]))
        out.append(("out1", 4, [("gla_w_out", PANEL * k, 2 * PANEL, 0, 4) for k in range(2)]))
    if upto >= 4:
        ffn(1)
    return out


class Chain:

    def __init__(self, engine, sem):
        self.engine, self.sem, self.base, self.here, self.i, self.per = engine, sem, 0, 0, 0, 0

    def __call__(self, ins):
        ins.then_inc(self.sem, 1)
        self.here += 1
        self.engine.wait_ge(self.sem, self.i * self.per + (self.base + self.here))

    @contextmanager
    def loop(self, count, per, start=0):
        assert self.here == 0 or self.per == 0
        self.base, self.here, self.per = self.base + self.here - start * per, 0, per
        with self.engine.Fori(start, start + count) as i:
            self.i = i
            yield i
        assert self.here == per, (self.here, per)
        self.base, self.here, self.i, self.per = self.base + (start + count) * per, 0, 0, 0


def trunk_kernel(nc, A, upto=4):
    ctx = ExitStack()
    with ctx:
        build(nc, ctx, A, upto)


def build(nc, ctx, A, upto):
    def sb(name, shape, dt=F32):
        return ctx.enter_context(nc.sbuf_tensor(name, shape, dt))

    def at(name, shape, host, offset, dt=F32):
        start, stop = host.manual_base
        size = int(np.prod(shape[1:])) * 4
        assert offset % 32 == 0 and start + offset + size <= stop, (name, offset, size, stop - start)
        return nc.alloc_sbuf_tensor_at(name, shape, dt, offset=start + offset)

    class Region:
        def __init__(self, name, shape, dt=F32):
            size = -(-int(np.prod(shape[1:])) * 4 // 32) * 32
            start = Region.top
            Region.top += size
            assert Region.top <= nc.sbuf_usable_end, (name, Region.top)
            self.manual_base = (start, start + size)
            self.t = nc.alloc_sbuf_tensor_at(name, shape, dt, offset=start)

        def __getitem__(self, k):
            return self.t[k]

    Region.top = -(-nc.sbuf_base // 32) * 32
    raw = Region("raw", [P, RAW_SLOTS, UNIT_KT, PANEL])
    w_hi = Region("w_hi", [P, SPLIT_SLOTS, UNIT_KT, PANEL], F32R)
    w_lo = Region("w_lo", [P, SPLIT_SLOTS, UNIT_KT, PANEL], F32R)
    h = Region("h", [P, KT, T])
    xs = Region("xs", [P, 2, KT, T])
    x_hi = at("x_hi", [P, KT, T], xs, 0, F32R)
    x_lo = at("x_lo", [P, KT, T], xs, KT * T * 4, F32R)
    y_hi = Region("y_hi", [P, KT, T], F32R)
    y_lo = Region("y_lo", [P, KT, T], F32R)
    mo = Region("mo", [P, KT, T])
    r1 = Region("r1", [P, 32, T])
    trunk_c = Region("trunk_c", [P, 3, P])
    params = Region("params", [P, PT_GROUPS * P])
    derived = Region("derived", [P, N_DCOLS + 2])
    rpre = Region("rpre", [P, T])
    small = Region("small", [P, 528])
    ident, ones, head_ones = trunk_c[:, 0, :], trunk_c[:, 1, :], trunk_c[:, 2, :]
    eps_col, gn_eps_col = derived[:, N_DCOLS:N_DCOLS + 1], derived[:, N_DCOLS + 1:N_DCOLS + 2]

    def par(name, i, count=1):
        return params[:, ds(COL[name] + i, count)]

    def der(name, i, count=1):
        return derived[:, ds(DCOL[name] + i, count)]

    TB = T * 4
    x_tok = at("x_tok", [P, 2, D_MODEL], r1, 0)
    meta_tok = at("meta_tok", [N_META, D_MODEL], r1, 16384)
    par_rows = at("par_rows", [P, PT_GROUPS, P], r1, 24576)
    acc = at("acc", [P, T], r1, 0)
    sq = at("sq", [P, 2, 2, T], r1, TB)
    root = at("root", [P, T], r1, 5 * TB)
    rpost = at("rpost", [P, T], r1, 6 * TB)
    gate_in = at("gate_in", [P, 2, T + 2], r1, 7 * TB + 0)
    conv = at("conv", [P, 2, T], r1, 10 * TB)
    gelu = at("gelu", [P, 2, T], r1, 12 * TB)
    val = at("val", [P, 2, T], r1, 14 * TB)
    prod = at("prod", [P, 2, T], r1, 16 * TB)
    rkv = at("rkv", [P, 24, T], r1, 0)
    lora = at("lora", [P, 2, T], r1, 24 * TB)
    gate_w = at("gate_w", [P, 4, P], r1, 28288)
    pair_w = at("pair_w", [P, 2, P], r1, 30336)
    state = at("state", [P, 5, P], r1, 31360)
    u_in = at("u_in", [P, 2, T + 1], mo, 0)
    lx_in = at("lx_in", [P, 2, T + 3], mo, 0)
    lx = at("lx", [P, 2, T], mo, 2208)
    rg = at("rg", [P, 2, T], mo, 4384)
    ig = at("ig", [P, 2, T], mo, 6560)
    aa = at("aa", [P, 2, T], mo, 8736)
    th = at("th", [P, 2, T], mo, 10912)
    ly = at("ly", [P, 2, T], mo, 13088)

    kk, inv, dk, ag, gg, cum, e_neg, e_pos, k2, rk = (at(f"pair{n}", [P, T], mo, n * TB) for n in range(10))
    ar = at("ar", [P, 2, T], mo, 10 * TB)
    beta = at("beta", [P, T], mo, 12 * TB)
    kappa = at("kappa", [P, T], mo, 13 * TB)
    beta_end = at("beta_end", [P, 2 * P], mo, 14 * TB)
    kappa_end = at("kappa_end", [P, 2 * P], mo, 15 * TB)
    rw_c = at("rw_c", [P, 1812], xs, 0)
    A4 = at("A4", [P, 2, 2, 2 * P], xs, 7264)
    B4 = at("B4", [P, 2, 2, 2 * P], xs, 11360)
    M4 = at("M4", [P, 4, P], xs, 15456)
    Z4 = at("Z4", [P, 4, P], xs, 17504)
    W4 = at("W4", [P, 4, P], xs, 19552)
    T4 = at("T4", [P, 4, P], xs, 21600)
    F4 = at("F4", [P, 4, P], xs, 23648)
    XX = at("XX", [P, 2, 2, 2, 64], xs, 25696)
    BX = at("BX", [P, 2, 2, 2, 64], xs, 27744)
    KX = at("KX", [P, 2, 2, 2, 64], xs, 29792)
    tXX = at("tXX", [TAIL, 2, 2, 64], xs, 31840)
    rq = at("rq", [P, T], xs, 32864)
    gbd = at("gbd", [P, 4, P], xs, 21600)
    dci = at("dci", [P, 4, 64], xs, 23648)
    v_tok = at("v_tok", [P, 2, P], small, 0)
    v_loc = at("v_loc", [P, T], small, 1024)
    tA = at("tA", [TAIL, 2, 2, TAIL], r1, 28288)
    tB = at("tB", [TAIL, 2, 2, TAIL], r1, 28544)
    tM, tZ, tW, tT, tF = (at(n, [TAIL, 2, TAIL], r1, 28800 + 128 * k) for k, n in enumerate(("tM", "tZ", "tW", "tT", "tF")))
    tV = at("tV", [TAIL, P], r1, 29440)
    MASK = {"A": 0, "B": 256, "M": 512, "pair": 640, "pairT": 768, "levels": 896, "chunk": 1536, "nchunk": 1538,
            "restart": 1540}

    def mask(name, n=P, rows=P):
        return rw_c[0:rows, MASK[name]:MASK[name] + n]


    qkv = at("qkv", [P, 32, T], r1, 0)
    g_all = at("g_all", [P, 16, T], mo, 0)
    gd_w = at("gd_w", [P, KT, 16], small, 0)
    gd_t = at("gd_t", [16, T], small, 1024)
    gl_c = at("gl_c", [P, 8, P], xs, 0)
    gk_w = at("gk_w", [16, GLA_DK], xs, 4096)
    q_loc = at("q_loc", [P, 2, T], xs, 5120)
    k_loc = at("k_loc", [P, 2, T], xs, 7296)
    v_all = at("v_all", [P, 4, T], xs, 9472)
    gk = at("gk", [P, 2, T], xs, 13824)
    gx = at("gx", [P, 2, T], xs, 16000)
    lev = at("lev", [P, 2, T], xs, 18176)
    v_rows = at("v_rows", [P, 3, GLA_DV], xs, 20352)
    at0 = at("at0", [P, T], xs, 26496)
    at1 = at("at1", [P, P + TAIL], xs, 27584)
    at2 = at("at2", [TAIL, TAIL], xs, 28160)
    part = at("part", [P, 2, P], xs, 28224)
    part2 = at("part2", [TAIL, TAIL], xs, 29248)
    gsq = at("gsq", [P, 4, T], xs, 29312)
    gr = at("gr", [P, T], xs, 33664)
    out_tok = at("out_tok", [P, 2, D_MODEL], xs, 0)

    main_ps = [ctx.enter_context(nc.psum_tensor(f"main{n}", [P, 2, 512], F32)) for n in range(2)]
    X = [ctx.enter_context(nc.psum_tensor(f"aux{n}", [P, 512], F32)) for n in range(4)]

    plan, FIRST, n = phases(upto), {}, 0
    PLAN = {name: (iters, panels) for name, iters, panels in plan}
    for name, iters, panels in plan:
        FIRST[name] = n
        n += iters * len(panels)
    TOTAL_UNITS = UNITS * n
    LAST_PHASE = plan[-1][0]
    views = {}
    for name in ("ab_w_in", "ab_w_out", "gla_w_in", "gla_w_out"):
        views[name] = A[name].rearrange("l (k p) n -> p (l k) n", p=P)
    for layer in range(2):
        for short, full in (("gate", "ffn_w_gate"), ("val", "ffn_w_val"), ("down", "ffn_w_down")):
            views[f"{short}{layer}"] = A[full][layer].rearrange("(k p) n -> p k n", p=P)

    def sem(name):
        return ctx.enter_context(nc.semaphore(name))

    def sems(names):
        return [sem(n) for n in names.split()]

    raw_landed = [sem(f"raw_landed{s}") for s in range(RAW_SLOTS)]
    drained = [sem("drained0"), sem("drained1")]
    hi_made, lo_made, unit_used = sems("hi_made lo_made unit_used")
    act_chain, dve_chain, pool_chain = sems("act_chain dve_chain pool_chain")
    inputs_landed, params_landed, trunk_landed, rwc_landed = sems(
        "inputs_landed params_landed trunk_landed rwc_landed")
    par_turned, params_ready, lam_exp = sems("par_turned params_ready lam_exp")
    h_turned, h_ready, x_hi_made, x_lo_made, h_squared = sems("h_turned h_ready x_hi_made x_lo_made h_squared")
    pre_sum, pre_root, squared, added, post_sum, post_root = sems("pre_sum pre_root squared added post_sum post_root")
    conv_made, gelu_made, prod_made, y_hi_made, y_lo_made = sems("conv_made gelu_made prod_made y_hi_made y_lo_made")
    gatew_landed, gates_summed, gates_made, lx_made, gatew_zeroed = sems(
        "gatew_landed gates_summed gates_made lx_made gatew_zeroed")
    lru_root_in, lru_root, decays_made, a2_made, lru_gelu, lru_made = sems(
        "lru_root_in lru_root decays_made a2_made lru_gelu lru_made")
    lora_in, lora_made = sems("lora_in lora_made")
    out_turned, out_copied, out_landed = sems("out_turned out_copied out_landed")

    def bank(n):
        return main_ps[n % 2][:, :, 0:T]

    def wide(ap, n=2):
        return ap.unsqueeze(1).broadcast_to([ap.shape[0], n, ap.shape[1]])

    Y_COUNT, y = {}, 0
    for name, add in [("out0", 12)] + [(f"dn0_{n}", FFN_PARTS[n][1]) for n in range(3)] + [("out1", 4)] + [
            (f"dn1_{n}", FFN_PARTS[n][1]) for n in range(3)]:
        y += add
        Y_COUNT[name] = y
    GV_COUNT = {"gv0_0": 0, "gv0_1": 8, "gv0_2": 16, "gv1_0": 22, "gv1_1": 30, "gv1_2": 38}
    SUBLAYERS = [("mix_pre", "mix_post", 0, "out0"), ("ffn_pre", "ffn_post", 0, "dn0_2"),
                 ("mix_pre", "mix_post", 1, "out1"), ("ffn_pre", "ffn_post", 1, "dn1_2")][:upto]

    def pre_w(s, m):
        return par(SUBLAYERS[s][0], m + KT * SUBLAYERS[s][2])

    def post_w(s, m):
        return par(SUBLAYERS[s][1], m + KT * SUBLAYERS[s][2])

    def iterations(engine, name, body):
        iters, _ = PLAN[name]
        if iters == 1:
            body(0)
            return
        end = iters - 1 if name == LAST_PHASE else iters
        with engine.Fori(0, end) as i:
            body(i)
        if name == LAST_PHASE:
            body(iters - 1)

    def wait_panel(engine, name, p, i):
        per = len(PLAN[name][1])
        engine.wait_ge(unit_used, i * (per * UNITS) + UNITS * (FIRST[name] + p + 1))

    def wait_drained(engine, name, p, i):
        n = FIRST[name] + p
        engine.wait_ge(drained[n % 2], i + (n // 2 + 1))

    (pairw_landed, lora_summed, lora_read, kq_made, kk_summed, kk_root, cum_made, lag_made, exps_made, rk_made,
     bonus_summed, bonus_read, v_loc_made, feats_made, rows_turned, rows_read_act, rows_read_dve, gram_made, gram_read,
     gram2_made, gram2_read, nv_summed, xx_made, moff_made, zw_made, t_summed, t_copied, zw_summed, wx_summed, wx_made,
     rq_summed, rq_made, g_summed, gbd_made, state_summed, state_made, y_summed, y_copied, mean_summed,
     ysq_made, var_summed, gn_root, pair_out) = sems(
        "pairw_landed lora_summed lora_read kq_made kk_summed kk_root cum_made lag_made exps_made rk_made "
        "bonus_summed bonus_read v_loc_made feats_made rows_turned rows_read_act rows_read_dve gram_made gram_read "
        "gram2_made gram2_read nv_summed xx_made moff_made zw_made t_summed t_copied zw_summed wx_summed wx_made "
        "rq_summed rq_made g_summed gbd_made state_summed state_made y_summed y_copied mean_summed "
        "ysq_made var_summed gn_root pair_out")
    PAIRS = RW // P
    NL = len(LEVELS)
    TAIL_LEVELS = sum(2 * size <= TAIL for size in LEVELS)
    HEAD = (slice(0, 64), slice(64, P))
    BLK = (slice(0, P), slice(P, 2 * P))
    END = slice(2 * P, T)

    def cols(q, n):
        return slice(q * n, (q + 1) * n)

    def rwkv_pe(pe, mm, turn):
        pe.wait_ge(lora_made, 1)
        with pe.Fori(0, PAIRS) as j:
            pe.wait_ge(y_lo_made, j + 4)
            pe.wait_ge(pairw_landed, j * 48 + 48)
            mm(X[0][:, 0:T], pair_w[0:64, 0, :], lora[0:64, 0, :])
            mm(X[1][:, 0:T], pair_w[64:P, 0, :], lora[64:P, 0, :])
            mm(X[2][:, 0:T], pair_w[:, 1, :], lora[:, 1, :]).then_inc(lora_summed, 1)
            pe.wait_ge(kq_made, j + 1)
            mm(X[3][:, 0:T], head_ones, inv[:]).then_inc(kk_summed, 1)
            pe.wait_ge(rk_made, j + 1)
            pe.wait_ge(lora_read, j + 1)
            mm(X[0][:, 0:T], head_ones, rk[:]).then_inc(bonus_summed, 1)
            pe.wait_ge(v_loc_made, j + 1)
            for b in range(2):
                turn(X[1][:, cols(b, P)], v_loc[:, BLK[b]])
            turn(X[1][0:TAIL, 256:384], v_loc[:, END])
            pe.wait_ge(feats_made, j + 1)
            for b in range(2):
                turn(X[2][:, cols(b, P)], ar[:, 0, BLK[b]])
            turn(X[2][0:TAIL, 256:384], ar[:, 0, END])
            for b in range(2):
                turn(X[3][:, cols(b, P)], beta_end[:, BLK[b]])
                ins = turn(X[3][:, cols(2 + b, P)], kappa_end[:, BLK[b]])
            ins.then_inc(rows_turned, 1)
            pe.wait_ge(rows_read_act, j + 1)
            pe.wait_ge(rows_read_dve, j + 1)
            pe.wait_ge(bonus_read, j + 1)
            for k, hs in enumerate(HEAD):
                for b in range(2):
                    mm(X[k][:, cols(b, 256)].rearrange("p (a t) -> p a t", a=2), kappa[hs, BLK[b]], ar[hs, :, BLK[b]])
                    ins = mm(X[2 + k][:, cols(b, 256)].rearrange("p (a t) -> p a t", a=2), beta[hs, BLK[b]],
                             ar[hs, :, BLK[b]])
            ins.then_inc(gram_made, 1)
            pe.wait_ge(gram_read, j + 1)
            for k, hs in enumerate(HEAD):
                for b in range(2):
                    mm(X[k][:, cols(b, P)], ar[hs, 0, BLK[b]], beta[hs, BLK[b]])
                tail = X[2 + k][0:TAIL]
                mm(tail[:, 0:32].rearrange("p (a t) -> p a t", a=2), kappa[hs, END], ar[hs, :, END])
                mm(tail[:, 32:64].rearrange("p (a t) -> p a t", a=2), beta[hs, END], ar[hs, :, END])
                ins = mm(tail[:, 64:80], ar[hs, 0, END], beta[hs, END])
            ins.then_inc(gram2_made, 1)
            pe.wait_ge(gram2_read, j + 1)
            for k, hs in enumerate(HEAD):
                for b in range(2):
                    mm(X[0][:, cols(2 * k + b, 64)], A4[:, k, b, 0:P], v_tok[:, b, hs])
                ins = mm(X[0][0:TAIL, cols(4 + k, 64)], tA[:, k, 0, :], tV[:, hs])
            ins.then_inc(nv_summed, 1)
            pe.wait_ge(xx_made, j + 1)
            for n in range(NL):
                pe.wait_ge(moff_made, j * NL + (n + 1))
                pe.wait_ge(zw_made, j * (NL + 1) + (n + 1))
                for q in range(4):
                    ins = mm(X[1][:, cols(q, P)], F4[:, q, :], Z4[:, q, :])
                if n < TAIL_LEVELS:
                    for k in range(2):
                        ins = mm(X[0][0:TAIL, cols(k, TAIL)], tF[:, k, :], tZ[:, k, :])
                ins.then_inc(t_summed, 1)
                pe.wait_ge(t_copied, j * NL + (n + 1))
                for q in range(4):
                    ins = mm(X[2][:, cols(q, P)], W4[:, q, :], T4[:, q, :])
                    if n < NL - 1:
                        ins = mm(X[3][:, cols(q, P)], T4[:, q, :], W4[:, q, :])
                if n < TAIL_LEVELS:
                    for k in range(2):
                        mm(X[0][0:TAIL, cols(2 + k, TAIL)], tW[:, k, :], tT[:, k, :])
                        ins = mm(X[0][0:TAIL, cols(4 + k, TAIL)], tT[:, k, :], tW[:, k, :])
                ins.then_inc(zw_summed, 1)
            pe.wait_ge(zw_made, j * (NL + 1) + (NL + 1))
            for k in range(2):
                for b in range(2):
                    mm(X[1][:, cols(2 * k + b, P)], Z4[:, 2 * k + b, :], XX[:, k, b])
                ins = mm(X[0][0:TAIL, cols(k, P)], tZ[:, k, :], tXX[:, k])
            ins.then_inc(wx_summed, 1)
            pe.wait_ge(wx_made, j + 1)
            for k, hs in enumerate(HEAD):
                for b in range(2):
                    mm(X[2][hs, BLK[b]], XX[:, k, b, 0, :], B4[:, k, b, P:2 * P])
                ins = mm(X[2][hs, END], tXX[:, k, 0, :], tB[:, k, 1, :])
            ins.then_inc(rq_summed, 1)
            for k, hs in enumerate(HEAD):
                for b in range(2):
                    ins = mm(X[3][hs, BLK[b]], XX[:, k, b, 0, :], BX[:, b, k])
            ins.then_inc(g_summed, 1)
            for k, hs in enumerate(HEAD):
                for b in range(2):
                    mm(X[0][hs, BLK[b]], v_tok[:, b, hs], A4[:, k, b, P:2 * P], start=(b == 0), stop=False)
                    mm(X[0][hs, BLK[b]], XX[:, k, b, 1, :], B4[:, k, b, P:2 * P], start=False, stop=False)
                mm(X[0][hs, END], tV[:, hs], tA[:, k, 1, :], start=False, stop=False)
                mm(X[0][hs, END], tXX[:, k, 1, :], tB[:, k, 1, :], start=False, stop=False)
            pe.wait_ge(gbd_made, j + 1)
            for c in range(4):
                b, half = divmod(c, 2)
                new = X[1][:, cols(c, P)]
                if c:
                    pe.wait_ge(state_made, j * 4 + c)
                mm(new, gbd[:, c, :], state[:, c, :], stop=False)
                for k, hs in enumerate(HEAD):
                    mm(new[hs, hs], KX[:, b, k, half, :], v_tok[:, b, hs], start=False, stop=False)
                    ins = mm(new[hs, hs], BX[:, b, k, half, :], XX[:, k, b, 1, :], start=False, stop=True)
                ins.then_inc(state_summed, 1)
            pe.wait_ge(state_made, j * 4 + 4)
            pe.wait_ge(rq_made, j + 1)
            for c in range(1, 5):
                t = slice(CH * c, min(CH * (c + 1), T))
                ins = mm(X[0][:, t], state[:, c, :], rq[:, t], start=False, stop=(c == 4))
            ins.then_inc(y_summed, 1)
            pe.wait_ge(y_copied, j + 1)
            mm(X[2][:, 0:T], head_ones, rk[:]).then_inc(mean_summed, 1)
            pe.wait_ge(ysq_made, j + 1)
            mm(X[3][:, 0:T], head_ones, inv[:]).then_inc(var_summed, 1)

    def rwkv_act(act, fn):
        with act.Fori(0, PAIRS) as j:
            act.wait_ge(lora_summed, j + 1)
            fn(dk[:], X[0][:, 0:T], ACT.Sigmoid, bias=par("w0", j))
            fn(ag[:], X[1][:, 0:T], ACT.Sigmoid, bias=par("a0", j))
            fn(gg[:], X[2][:, 0:T], ACT.Copy).then_inc(lora_read, 1)
            act.wait_ge(kk_summed, j + 1)
            fn(inv[:], X[3][:, 0:T], ACT.Sqrt).then_inc(kk_root, 1)
            act.wait_ge(cum_made, j + 1)
            fn(e_neg[:], cum[:], ACT.Exp, scale=-DECAY)
            fn(e_pos[:], cum[:], ACT.Exp, scale=DECAY)
            act.wait_ge(lag_made, j + 1)
            fn(dk[:], dk[:], ACT.Exp, scale=-DECAY).then_inc(exps_made, 1)
            act.wait_ge(rows_turned, j + 1)
            fn(v_tok[:], X[1][:, 0:256].rearrange("p (a t) -> p a t", a=2), ACT.Copy)
            fn(tV[:], X[1][0:TAIL, 256:384], ACT.Copy).then_inc(rows_read_act, 1)
            for n in range(NL):
                act.wait_ge(t_summed, j * NL + (n + 1))
                ins = fn(T4[:], X[1][:].rearrange("p (a t) -> p a t", a=4), ACT.Copy)
                if n < TAIL_LEVELS:
                    ins = fn(tT[:], X[0][0:TAIL, 0:32].rearrange("p (a t) -> p a t", a=2), ACT.Copy)
                ins.then_inc(t_copied, 1)
            for c in range(4):
                act.wait_ge(state_summed, j * 4 + (c + 1))
                fn(state[:, c + 1, :], X[1][:, cols(c, P)], ACT.Copy).then_inc(state_made, 1)
            act.wait_ge(y_summed, j + 1)
            fn(rk[:], X[0][:, 0:T], ACT.Copy).then_inc(y_copied, 1)
            act.wait_ge(var_summed, j + 1)
            fn(inv[:], X[3][:, 0:T], ACT.Sqrt, scale=1.0 / 64, bias=gn_eps_col).then_inc(gn_root, 1)
            act.wait_ge(pair_out, j + 1)
            fn(y_hi[:, 8 + j, :], dk[:], ACT.Copy).then_inc(y_hi_made, 1)

    def rwkv_pool(pool):
        def weights(j):
            c = ds(j * P, P)
            pool.dma_start(pair_w[0:64, 0, :], A["rwkv_w2"][0][:, c]).then_inc(pairw_landed, 16)
            pool.dma_start(pair_w[64:P, 0, :], A["rwkv_a2"][0][:, c]).then_inc(pairw_landed, 16)
            pool.dma_start(pair_w[:, 1, :], A["rwkv_g2"][0][:, c]).then_inc(pairw_landed, 16)

        def pair(j):
            pool.wait_ge(y_lo_made, j + 4)
            pool.tensor_copy(v_loc[:], rkv[:, 16 + j, :]).then_inc(v_loc_made, 1)
            pool.wait_ge(gram2_read, j + 1)
            for n in range(NL):
                if n:
                    pool.wait_ge(t_summed, j * NL + n)
                level = rw_c[:, MASK["levels"] + n * P:MASK["levels"] + (n + 1) * P]
                ins = pool.tensor_tensor(F4[:], M4[:], wide(level, 4), ALU.mult)
                if n < TAIL_LEVELS:
                    ins = pool.tensor_tensor(tF[:], tM[:], wide(level[0:TAIL, 0:TAIL], 2), ALU.mult)
                ins.then_inc(moff_made, 1)

        pool.wait_ge(unit_used, UNITS * FIRST["out0"])
        pool.dma_start(rw_c[:], A["const_rwkv"]).then_inc(rwc_landed, 16)
        pool.wait_ge(rwc_landed, 16)
        weights(0)
        with pool.Fori(0, PAIRS - 1) as j:
            pool.wait_ge(lora_summed, j + 1)
            weights(j + 1)
            pair(j)
        pair(PAIRS - 1)

    def rwkv_dve(dve, link, tt, stt, ts, split_y):
        copy = nc.vector.tensor_copy
        link(nc.vector.memset(state[:, 0, :], 0.0))
        dve.wait_ge(rwc_landed, 16)
        ends = slice(CH - 1, 4 * CH, CH)
        with link.loop(PAIRS, RWKV_STEPS) as j:
            r, k, v = rkv[:, j, :], rkv[:, j + 8, :], rkv[:, j + 16, :]
            link(ts(kk[:], k, par("k_k", j), None, ALU.mult))
            tt(inv[:], kk[:], kk[:], ALU.mult).then_inc(kq_made, 1)
            dve.wait_ge(lora_read, j + 1)
            nc.vector.tensor_tensor_scan(cum[:], mask("restart", T), dk[:], 0.0, ALU.mult, ALU.add).then_inc(cum_made, 1)
            dve.wait_ge(cum_made, j + 1)
            tt(dk[:], cum[:], dk[:], ALU.subtract).then_inc(lag_made, 1)
            link(ts(k2[:], ag[:], par("k_a", j), der("one_minus_ka", j), ALU.mult, ALU.add))
            link(tt(k2[:], k2[:], k, ALU.mult))
            stt(rk[:], r, par("r_k", j), k2[:], ALU.mult, ALU.mult).then_inc(rk_made, 1)
            dve.wait_ge(kk_root, j + 1)
            link(ts(inv[:], inv[:], 1e-12, None, ALU.max))
            link(nc.vector.reciprocal(inv[:], inv[:]))
            link(tt(kk[:], kk[:], inv[:], ALU.mult))
            dve.wait_ge(exps_made, j + 1)
            tt(ar[:, 0, :], kk[:], dk[:], ALU.mult)
            tt(ar[:, 1, :], r, e_neg[:], ALU.mult)
            link(tt(inv[:], kk[:], ag[:], ALU.mult))
            tt(beta[:], inv[:], e_pos[:], ALU.mult)
            link(tt(kappa[:], k2[:], e_pos[:], ALU.mult))
            whole = e_neg[:, ends].unsqueeze(2).broadcast_to([P, 4, CH])

            def chunked(ap):
                return ap.rearrange("p (c t) -> p c t", t=CH)
            tt(chunked(beta_end[:]), chunked(beta[:, 0:256]), whole, ALU.mult)
            tt(chunked(kappa_end[:]), chunked(kappa[:, 0:256]), whole, ALU.mult).then_inc(feats_made, 1)
            dve.wait_ge(bonus_summed, j + 1)
            tt(cum[:], X[0][:, 0:T], v, ALU.mult).then_inc(bonus_read, 1)
            dve.wait_ge(rows_turned, j + 1)
            for b in range(2):
                copy(XX[:, :, b, 0, :], X[2][:, cols(b, P)].rearrange("p (a t) -> p a t", a=2))
            copy(tXX[:, :, 0, :], X[2][0:TAIL, 256:384].rearrange("p (a t) -> p a t", a=2))

            def by_chunk(ap):
                return ap.rearrange("p (q v) -> p q v", q=4).unsqueeze(2).broadcast_to([P, 4, 2, 64])

            def chunk_mask(name):
                return mask(name, 2).unsqueeze(1).unsqueeze(3).broadcast_to([P, 4, 2, 64])
            tt(BX[:].rearrange("p b k c v -> p (b k) c v"), by_chunk(X[3][:, 0:256]), chunk_mask("nchunk"), ALU.mult)
            tt(KX[:].rearrange("p b k c v -> p (b k) c v"), by_chunk(X[3][:, 256:512]), chunk_mask("chunk"),
               ALU.mult).then_inc(rows_read_dve, 1)
            dve.wait_ge(gram_made, j + 1)
            for k_ in range(2):
                tt(A4[:, k_], X[k_][:].rearrange("p (a t) -> p a t", a=2), wide(mask("A", 256)), ALU.mult)
                ins = tt(B4[:, k_], X[2 + k_][:].rearrange("p (a t) -> p a t", a=2), wide(mask("B", 256)), ALU.mult)
            ins.then_inc(gram_read, 1)
            dve.wait_ge(gram2_made, j + 1)
            for k_ in range(2):
                tt(M4[:, 2 * k_:2 * k_ + 2, :], X[k_][:, 0:256].rearrange("p (a t) -> p a t", a=2), wide(mask("M")), ALU.mult)
                tail = X[2 + k_][0:TAIL]
                for dst, c, name in ((tA, 0, "A"), (tB, 32, "B")):
                    m = mask(name, 256, TAIL).rearrange("p (a t) -> p a t", a=2)[:, :, 0:TAIL]
                    tt(dst[:, k_], tail[:, c:c + 32].rearrange("p (a t) -> p a t", a=2), m, ALU.mult)
                ins = tt(tM[:, k_, :], tail[:, 64:80], mask("M", TAIL, TAIL), ALU.mult)
            ins.then_inc(gram2_read, 1)
            dve.wait_ge(gram2_read, j + 1)
            E4 = B4[:].rearrange("p k b t -> p (k b) t")[:, :, 0:P]
            tt(W4[:], M4[:], wide(mask("pair"), 4), ALU.mult)
            tt(Z4[:], E4, wide(mask("pairT"), 4), ALU.mult)
            tt(tW[:], tM[:], wide(mask("pair", TAIL, TAIL)), ALU.mult)
            link(tt(tZ[:], tB[:, :, 0, :], wide(mask("pairT", TAIL, TAIL)), ALU.mult))
            tt(W4[:], wide(ident, 4), W4[:], ALU.subtract)
            tt(Z4[:], wide(ident, 4), Z4[:], ALU.subtract)
            tt(tW[:], wide(ident[0:TAIL, 0:TAIL]), tW[:], ALU.subtract)
            tt(tZ[:], wide(ident[0:TAIL, 0:TAIL]), tZ[:], ALU.subtract).then_inc(zw_made, 1)
            dve.wait_ge(nv_summed, j + 1)
            copy(XX[:].rearrange("p k b a v -> p (k b) a v")[:, :, 1, :], X[0][:, 0:256].rearrange("p (q v) -> p q v", q=4))
            copy(tXX[:, :, 1, :], X[0][0:TAIL, 256:384].rearrange("p (q v) -> p q v", q=2)).then_inc(xx_made, 1)
            for n in range(NL):
                dve.wait_ge(zw_summed, j * NL + (n + 1))
                dve.wait_ge(zw_made, j * (NL + 1) + (n + 1))
                ins = tt(Z4[:], Z4[:], X[2][:].rearrange("p (a t) -> p a t", a=4), ALU.subtract)
                if n < NL - 1:
                    ins = tt(W4[:], W4[:], X[3][:].rearrange("p (a t) -> p a t", a=4), ALU.subtract)
                if n < TAIL_LEVELS:
                    tt(tZ[:], tZ[:], X[0][0:TAIL, 32:64].rearrange("p (a t) -> p a t", a=2), ALU.subtract)
                    ins = tt(tW[:], tW[:], X[0][0:TAIL, 64:96].rearrange("p (a t) -> p a t", a=2), ALU.subtract)
                ins.then_inc(zw_made, 1)
            dve.wait_ge(wx_summed, j + 1)
            copy(XX[:].rearrange("p k b a v -> p (k b a v)"), X[1][:])
            copy(tXX[:].rearrange("p k a v -> p (k a v)"), X[0][0:TAIL, 0:256]).then_inc(wx_made, 1)
            nc.vector.memset(gbd[:], 0.0)
            for hs in HEAD:
                ins = tt(dci[hs], wide(ident[hs, hs], 4), e_neg[hs, ends].unsqueeze(2).broadcast_to([64, 4, 64]), ALU.mult)
            link(ins)
            dve.wait_ge(rq_summed, j + 1)
            tt(rq[:], ar[:, 1, :], X[2][:, 0:T], ALU.add).then_inc(rq_made, 1)
            dve.wait_ge(g_summed, j + 1)
            for hs in HEAD:
                ins = tt(gbd[hs, :, hs], X[3][hs, 0:256].rearrange("p (c t) -> p c t", c=4), dci[hs], ALU.add)
            ins.then_inc(gbd_made, 1)
            dve.wait_ge(mean_summed, j + 1)
            link(stt(kk[:], X[2][:, 0:T], -1.0 / 64, rk[:], ALU.mult, ALU.add))
            tt(inv[:], kk[:], kk[:], ALU.mult).then_inc(ysq_made, 1)
            dve.wait_ge(gn_root, j + 1)
            link(nc.vector.reciprocal(inv[:], inv[:]))
            link(tt(kk[:], kk[:], inv[:], ALU.mult))
            link(ts(kk[:], kk[:], par("ln_w", j), par("ln_b", j), ALU.mult, ALU.add))
            link(tt(kk[:], kk[:], cum[:], ALU.add))
            tt(dk[:], kk[:], gg[:], ALU.mult).then_inc(pair_out, 1)
            split_y(8 + j, dk[:], j + 5)

    RWKV_STEPS = 15

    (glc_landed, gdw_landed, gdw_made, gd_summed, gd_made, gkw_landed, gk_summed, logits_made, soft_made, gk_made, qkv_copied,
     v_turned, v_rows_made, diff_made, lev_exp, lev_made, score_summed, score_read, parts_added, o_summed, o_copied,
     on_summed, on_root, silu_made, o_made) = sems(
        "glc_landed gdw_landed gdw_made gd_summed gd_made gkw_landed gk_summed logits_made soft_made gk_made qkv_copied "
        "v_turned v_rows_made diff_made lev_exp lev_made score_summed score_read parts_added o_summed o_copied "
        "on_summed on_root silu_made o_made")
    HEADS = GLA_KW // GLA_DK
    SIZES = GLA_LEVELS + (P, 2 * P)
    NS = len(SIZES) + 1
    Y0 = 12 + 22

    def lev_at(s):
        return lev[:] if s % 2 == 0 else gsq[:, 0:2, :]

    def diff_at(s):
        return gx[:] if s % 2 == 0 else gsq[:, 2:4, :]

    def halves(ap, size):
        if size == 2 * P:
            left, right, ref = ap[:, :, 0:size], ap[:, :, size:T], ap[:, :, size - 1:size]
            return (left, ref.broadcast_to([P, 2, size])), (right, ref.broadcast_to([P, 2, TAIL]))
        n = (T if 2 * size <= TAIL else 2 * P) // (2 * size)
        v = ap[:, :, 0:n * 2 * size].rearrange("p d (n a t) -> p d n a t", a=2, t=size)
        ref = v[:, :, :, 0, size - 1:size].broadcast_to([P, 2, n, size])
        return (v[:, :, :, 0, :], ref), (v[:, :, :, 1, :], ref)

    def gla_pe(pe, mm, turn):
        pe.wait_ge(gdw_made, 1)
        for k in range(KT):
            ins = mm(X[0][0:16, 0:T], gd_w[:, k, :], h[:, k, :], start=(k == 0), stop=(k == KT - 1))
        ins.then_inc(gd_summed, 1)
        pe.wait_ge(gd_made, 1)
        with pe.Fori(0, HEADS) as hd:
            pe.wait_ge(y_lo_made, hd + Y0)
            pe.wait_ge(gkw_landed, hd * 16 + 16)
            for n in range(2):
                ins = mm(X[n][:, 0:T], gk_w[:, cols(n, P)], gd_t[:])
            ins.then_inc(gk_summed, 1)
            pe.wait_ge(qkv_copied, hd + 1)
            for b in range(2):
                for m in range(4):
                    ins = turn(X[2 + b][:, cols(m, P)], v_all[:, m, BLK[b]])
            pe.wait_ge(logits_made, hd + 1)
            for m in range(4):
                ins = turn(X[0][0:TAIL, cols(m, P)], v_all[:, m, END])
            ins.then_inc(v_turned, 1)
            pe.wait_ge(v_rows_made, hd + 1)
            for s in range(NS):
                out = X[2 + s % 2]
                if s:
                    pe.wait_ge(lev_made, hd * (NS - 1) + s)
                    left = right = lev_at(s)
                else:
                    left, right = k_loc[:], q_loc[:]
                if s > 1:
                    pe.wait_ge(score_read, hd * NS + (s - 1))
                size = SIZES[s - 1] if s else 0
                if size == 2 * P:
                    places = [(out[:, 0:TAIL], BLK[0], END), (out[:, TAIL:2 * TAIL], BLK[1], END)]
                elif size == P:
                    places = [(out[:, 0:P], BLK[0], BLK[1])]
                else:
                    places = [(out[:, 0:P], BLK[0], BLK[0]), (out[:, P:2 * P], BLK[1], BLK[1])]
                    if 2 * size <= TAIL:
                        places.append((out[0:TAIL, 2 * P:2 * P + TAIL], END, END))
                for dst, sb_, tb in places:
                    for d in range(2):
                        ins = mm(dst, left[:, d, sb_], right[:, d, tb], start=(d == 0), stop=(d == 1))
                ins.then_inc(score_summed, 1)
            pe.wait_ge(score_read, hd * NS + NS)
            pe.wait_ge(parts_added, hd * len(GLA_LEVELS) + len(GLA_LEVELS))
            for m in range(4):
                mm(X[m][:, 0:T], v_rows[:, 0, cols(m, P)], at0[:], stop=False)
                mm(X[m][:, P:T], v_rows[:, 1, cols(m, P)], at1[:], start=False, stop=False)
                ins = mm(X[m][:, END], v_rows[0:TAIL, 2, cols(m, P)], at2[:], start=False)
            ins.then_inc(o_summed, 1)
            pe.wait_ge(o_copied, hd + 1)
            for m in range(4):
                ins = mm(X[0][:, 0:T], ones, gsq[:, m, :], start=(m == 0), stop=(m == 3))
            ins.then_inc(on_summed, 1)

    def gla_act(act, fn):
        with act.Fori(0, HEADS) as hd:
            act.wait_ge(logits_made, hd + 1)
            for f, k in ((ACT.Abs, {}), (ACT.Exp, {"scale": -1.0}), (ACT.Ln, {"bias": 1.0})):
                src = gx if f is ACT.Abs else lev
                fn(lev[:], src[:], f, **k).then_inc(soft_made, 1)
                act.wait_ge(soft_made, hd * 3 + {ACT.Abs: 1, ACT.Exp: 2, ACT.Ln: 3}[f])
            act.wait_ge(v_turned, hd + 1)
            for b in range(2):
                fn(v_rows[:, b, :], X[2 + b][:], ACT.Copy)
            fn(v_rows[0:TAIL, 2, :], X[0][0:TAIL, :], ACT.Copy).then_inc(v_rows_made, 1)
            for s in range(1, NS):
                act.wait_ge(diff_made, hd * (NS - 1) + s)
                if s > 2:
                    act.wait_ge(score_summed, hd * NS + (s - 1))
                n = T if 2 * SIZES[s - 1] <= TAIL or SIZES[s - 1] == 2 * P else 2 * P
                fn(lev_at(s)[:, :, 0:n], diff_at(s)[:, :, 0:n], ACT.Exp, scale=1.0 / 16).then_inc(lev_exp, 1)
            act.wait_ge(o_summed, hd + 1)
            for m in range(4):
                fn(v_all[:, m, :], X[m][:, 0:T], ACT.Copy)
                ins = fn(gsq[:, m, :], X[m][:, 0:T], ACT.Square)
            ins.then_inc(o_copied, 1)
            act.wait_ge(on_summed, hd + 1)
            fn(gr[:], X[0][:, 0:T], ACT.Sqrt, scale=1.0 / GLA_DV, bias=eps_col).then_inc(on_root, 1)
            fn(gsq[:], g_all[:, ds(hd * 4, 4), :], ACT.Silu).then_inc(silu_made, 1)
            act.wait_ge(o_made, hd + 1)
            fn(y_hi[:, ds(hd * 4, 4), :], v_all[:], ACT.Copy).then_inc(y_hi_made, 1)

    def gla_pool(pool):
        pool.dma_start(gd_w[:], A["gla_w_in"][0].rearrange("(k p) n -> p k n", p=P)[:, :, 2 * GLA_KW + 2 * GLA_VW:]).then_inc(
            gdw_landed, 16)
        pool.wait_ge(unit_used, UNITS * FIRST["out1"])
        pool.dma_start(gl_c[:], A["const_gla"].rearrange("p (a b) -> p a b", a=8)).then_inc(glc_landed, 16)
        pool.wait_ge(glc_landed, 16)

        def weights(hd):
            pool.dma_start(gk_w[:], A["gla_gk_up"][0][:, ds(hd * GLA_DK, GLA_DK)]).then_inc(gkw_landed, 16)

        def head(hd, last):
            pool.wait_ge(y_lo_made, hd + Y0)
            pool.tensor_copy(q_loc[:], qkv[:, ds(hd * 2, 2), :])
            pool.tensor_copy(k_loc[:], qkv[:, ds(hd * 2 + 8, 2), :])
            pool.tensor_copy(v_all[:], qkv[:, ds(hd * 4 + 16, 4), :]).then_inc(qkv_copied, 1)
            pool.wait_ge(gk_made, hd * 2 + 2)
            if not last:
                weights(hd + 1)

            def add(s):
                pool.wait_ge(score_read, hd * NS + (s + 1))
                pool.tensor_tensor(at0[:, 0:P], at0[:, 0:P], part[:, 0, :], ALU.add)
                ins = pool.tensor_tensor(at1[:, 0:P], at1[:, 0:P], part[:, 1, :], ALU.add)
                if 2 * SIZES[s - 1] <= TAIL:
                    ins = pool.tensor_tensor(at2[:], at2[:], part2[:], ALU.add)
                ins.then_inc(parts_added, 1)

            for s in range(1, NS):
                if s > 2:
                    pool.wait_ge(lev_exp, hd * (NS - 1) + (s - 2))
                (left, ref), (right, ref_r) = halves(gk[:], SIZES[s - 1])
                (dl, _), (dr, _) = halves(diff_at(s), SIZES[s - 1])
                for d in range(2):
                    pool.tensor_tensor(dl[:, d], ref[:, d], left[:, d], ALU.subtract)
                    ins = pool.tensor_tensor(dr[:, d], right[:, d], ref_r[:, d], ALU.subtract)
                ins.then_inc(diff_made, 1)
                if 2 <= s <= len(GLA_LEVELS) + 1:
                    if s > 2:
                        pool.wait_ge(parts_added, hd * len(GLA_LEVELS) + (s - 2))
                    add(s - 1)

        weights(0)
        with pool.Fori(0, HEADS - 1) as hd:
            head(hd, False)
        head(HEADS - 1, True)

    def gla_dve(dve, link, tt, stt, ts, split_y):
        dve.wait_ge(gd_summed, 1)
        tt(gd_t[:], X[0][0:16, 0:T], rpre[0:16, :], ALU.mult).then_inc(gd_made, 1)
        dve.wait_ge(glc_landed, 16)
        NG = len(GLA_LEVELS)
        with link.loop(HEADS, GLA_STEPS) as hd:
            dve.wait_ge(gk_summed, hd + 1)
            for n in range(2):
                ins = ts(gx[:, n, :], X[n][:, 0:T], par("gk_b", hd * 2 + n), None, ALU.add)
            ins.then_inc(logits_made, 1)
            dve.wait_ge(soft_made, hd * 3 + 3)
            link(stt(lev[:], gx[:], 0.0, lev[:], ALU.min, ALU.subtract))
            for n in range(2):
                nc.vector.tensor_tensor_scan(gk[:, n, :], ones[:, 0:1].broadcast_to([P, T]), lev[:, n, :], 0.0,
                                             ALU.mult, ALU.add).then_inc(gk_made, 1)

            def drain(s):
                dve.wait_ge(score_summed, hd * NS + (s + 1))
                src = X[2 + s % 2]
                size = SIZES[s - 1] if s else 0
                if size == 2 * P:
                    ts(at0[:, END], src[:, 0:TAIL], GLA_DK ** -0.5, None, ALU.mult)
                    ts(at1[:, P:P + TAIL], src[:, TAIL:2 * TAIL], GLA_DK ** -0.5, None, ALU.mult).then_inc(score_read, 1)
                    return
                if size == P:
                    ts(at0[:, BLK[1]], src[:, 0:P], GLA_DK ** -0.5, None, ALU.mult).then_inc(score_read, 1)
                    return
                m = gl_c[:, s, :]
                if s == 0:
                    tt(at0[:, 0:P], src[:, 0:P], m, ALU.mult)
                    tt(at1[:, 0:P], src[:, P:2 * P], m, ALU.mult)
                    tt(at2[:], src[0:TAIL, 2 * P:2 * P + TAIL], m[0:TAIL, 0:TAIL], ALU.mult).then_inc(score_read, 1)
                    return
                if s > 1:
                    dve.wait_ge(parts_added, hd * NG + (s - 1))
                if 2 * size <= TAIL:
                    tt(part2[:], src[0:TAIL, 2 * P:2 * P + TAIL], m[0:TAIL, 0:TAIL], ALU.mult)
                tt(part[:], src[:, 0:2 * P].rearrange("p (a t) -> p a t", a=2), wide(m), ALU.mult).then_inc(score_read, 1)

            dve.wait_ge(qkv_copied, hd + 1)
            for s in range(1, NS):
                dve.wait_ge(lev_exp, hd * (NS - 1) + s)
                (ll, _), (lr, _) = halves(lev_at(s), SIZES[s - 1])
                (kl, _), _ = halves(k_loc[:], SIZES[s - 1])
                _, (qr, _) = halves(q_loc[:], SIZES[s - 1])
                tt(ll, ll, kl, ALU.mult)
                tt(lr, lr, qr, ALU.mult).then_inc(lev_made, 1)
                drain(s - 1)
            drain(NS - 1)
            dve.wait_ge(on_root, hd + 1)
            link(nc.vector.reciprocal(gr[:], gr[:]))
            link(tt(v_all[:], v_all[:], wide(gr[:], 4), ALU.mult))
            dve.wait_ge(silu_made, hd + 1)
            for m in range(4):
                ins = stt(v_all[:, m, :], v_all[:, m, :], par("gla_nw", m), gsq[:, m, :], ALU.mult, ALU.mult)
            ins.then_inc(o_made, 1)
            split_y(ds(hd * 4, 4), v_all[:], hd + (Y0 + 1))

    GLA_STEPS = 3

    block = ctx.enter_context(nc.Block())

    @block.sync
    def _(sp):
        sp.dma_start(trunk_c[:], A["const_trunk"].rearrange("p (a b) -> p a b", a=3)).then_inc(trunk_landed, 16)
        sp.dma_start(x_tok[:], A["x"][0].rearrange("(b p) d -> p b d", p=P)).then_inc(inputs_landed, 16)
        sp.dma_start(meta_tok[:], A["meta_tokens"]).then_inc(inputs_landed, 16)

        for name, iters, panels in plan:
            first, per = FIRST[name] * UNITS, len(panels) * UNITS

            def iteration(i):
                for p, (w, c0, step, k0, kn) in enumerate(panels):
                    for u in range(UNITS):
                        unit = first + p * UNITS + u
                        slot = unit % RAW_SLOTS
                        if not isinstance(i, int):
                            sp.wait_ge(lo_made, i * per + (unit - RAW_SLOTS + 1))
                        elif unit + per * i >= RAW_SLOTS:
                            sp.wait_ge(lo_made, unit + per * i - RAW_SLOTS + 1)
                        k = k0 // P + u * kn
                        sp.dma_start(raw[:, slot, 0:kn, :],
                                     views[w][:, k:k + kn, ds(i * step + c0, PANEL)]).then_inc(raw_landed[slot], 16)

            start = 0
            while start < iters and first + start * per < RAW_SLOTS:
                iteration(start)
                start += 1
            if iters > start:
                with sp.Fori(start, iters) as i:
                    iteration(i)

        for b in range(2):
            sp.wait_ge(out_copied, 4 * (b + 1))
            sp.dma_start(A["out"][0, b * P:(b + 1) * P, :], out_tok[:, b, :]).then_inc(out_landed, 16)
        sp.wait_ge(out_landed, 32)

    def make_hi(act, unit, i, per):
        if isinstance(i, int):
            unit, i = unit + per * i, 0
            if unit >= TOTAL_UNITS:
                return
        slot = unit % RAW_SLOTS
        act.wait_ge(raw_landed[slot], i * (16 * per // RAW_SLOTS) + 16 * (unit // RAW_SLOTS + 1))
        if unit >= SPLIT_SLOTS:
            act.wait_ge(unit_used, i * per + (unit - SPLIT_SLOTS + 1))
        nc.scalar.activation(w_hi[:, unit % SPLIT_SLOTS], raw[:, slot], ACT.Copy).then_inc(hi_made, 1)

    def make_lo(dve, unit, i, per):
        if isinstance(i, int):
            unit, i = unit + per * i, 0
            if unit >= TOTAL_UNITS:
                return
        dve.wait_ge(hi_made, i * per + (unit + 1))
        nc.vector.tensor_tensor(w_lo[:, unit % SPLIT_SLOTS], raw[:, unit % RAW_SLOTS],
                                w_hi[:, unit % SPLIT_SLOTS].bitcast(F32), ALU.subtract).then_inc(lo_made, 1)

    def split_ahead(make, engine, name, p, i):
        per = len(PLAN[name][1])
        for u in range(3, 3 + UNITS):
            make(engine, UNITS * (FIRST[name] + p) + u, i, per * UNITS)

    @block.tensor
    def _(pe):
        def mm(out, lhsT, rhs, start=True, stop=True, **k):
            return nc.tensor.matmul(out, lhsT, rhs, start=start, stop=stop, **k)

        def turn(out, in_, rows=P):
            return nc.tensor.transpose(out, in_, trunk_c[0:rows, 0, 0:rows])

        def stream(name, hi, lo, after=None):
            _, panels = PLAN[name]
            per = len(panels)

            def body(i):
                for p in range(per):
                    kn = panels[p][4]
                    n, j = FIRST[name] + p, i
                    if isinstance(i, int):
                        n, j = n + per * i, 0
                    ps = main_ps[n % 2]
                    if n >= 2:
                        pe.wait_ge(drained[n % 2], j + n // 2)
                    for u in range(UNITS):
                        unit = UNITS * n + u
                        pe.wait_ge(lo_made, j * (per * UNITS) + (unit + 1))
                        for m in range(2):
                            for k in range(kn):
                                for a, b in ((w_hi, hi), (w_lo, hi), (w_hi, lo)):
                                    ins = mm(ps[:, m, 0:T], a[:, unit % SPLIT_SLOTS, k, m * P:(m + 1) * P],
                                             b[:, u * kn + k, :],
                                             start=(u == 0 and k == 0 and a is w_hi and b is hi),
                                             stop=(u == UNITS - 1 and k == kn - 1 and b is lo))
                        ins.then_inc(unit_used, 1)
                if after:
                    after(i)

            iterations(pe, name, body)

        def transition(t):
            if t > 0:
                pe.wait_ge(added, 20 * t)
                mm(X[0][:, 0:T], ones, acc[:]).then_inc(post_sum, 1)
            if t < upto:
                def tile(m, start, stop):
                    pe.wait_ge(h_squared, m + (KT * t + 1))
                    ins = mm(X[1][:, 0:T], ones, mo[:, m, :], start=start, stop=stop)
                    if stop:
                        ins.then_inc(pre_sum, 1)
                tile(0, True, False)
                with pe.Fori(1, KT - 1) as m:
                    tile(m, False, False)
                tile(KT - 1, False, True)
                pe.wait_ge(x_lo_made, KT * (t + 1))

        pe.wait_ge(trunk_landed, 16)
        pe.wait_ge(params_landed, 16 * N_PARAM_DMAS)
        for g in range(PT_GROUPS):
            ins = turn(X[g // 4][:, (g % 4) * P:(g % 4 + 1) * P], par_rows[:, g, :])
        ins.then_inc(par_turned, 1)
        pe.wait_ge(inputs_landed, 32)
        for k in range(KT):
            dst = X[2 + k % 2]
            if k >= 2:
                pe.wait_ge(h_ready, k - 1)
            cols = slice(k * P, (k + 1) * P)
            turn(dst[:, 0:N_META], meta_tok[:, cols], N_META)
            turn(dst[:, N_META:N_META + P], x_tok[:, 0, cols])
            turn(dst[:, N_META + P:T], x_tok[:, 1, cols]).then_inc(h_turned, 1)
        pe.wait_ge(params_ready, 1)
        transition(0)

        stream("wag", x_hi, x_lo)
        stream("rkv", x_hi, x_lo)

        def lru_gates(i):
            pe.wait_ge(gatew_landed, i * 64 + 64)
            pe.wait_ge(lx_made, i + 1)
            for n in range(4):
                ins = mm(X[n][:, 0:T], gate_w[:, n, :], lx[:, n % 2, :])
            ins.then_inc(gates_summed, 1)

        stream("lru", x_hi, x_lo, lru_gates)
        rwkv_pe(pe, mm, turn)
        pe.wait_ge(y_lo_made, Y_COUNT["out0"])
        stream("out0", y_hi, y_lo)
        transition(1)

        def ffn(layer):
            for n in range(3):
                stream(f"gv{layer}_{n}", x_hi, x_lo)
                pe.wait_ge(y_lo_made, Y_COUNT[f"dn{layer}_{n}"])
                stream(f"dn{layer}_{n}", y_hi, y_lo)
            transition(2 * layer + 2)

        if upto >= 2:
            ffn(0)
        if upto >= 3:
            stream("gla_qkv", x_hi, x_lo)
            stream("gla_g", x_hi, x_lo)
            gla_pe(pe, mm, turn)
            pe.wait_ge(y_lo_made, Y_COUNT["out1"])
            stream("out1", y_hi, y_lo)
            transition(3)
        if upto >= 4:
            ffn(1)
        pe.wait_ge(h_ready, KT * (upto + 1))
        for b in range(2):
            for g in range(4):
                n = 4 * b + g
                if n >= 4:
                    pe.wait_ge(out_copied, n - 3)
                for k in range(4):
                    c = N_META + b * P
                    ins = turn(X[g][:, k * P:(k + 1) * P], h[:, 4 * g + k, c:c + P])
                ins.then_inc(out_turned, 1)

    @block.scalar
    def _(act):
        link = Chain(act, act_chain)

        def fn(out, in_, f, **k):
            return nc.scalar.activation(out, in_, f, **k)

        def stream(name, drain):
            def body(i):
                for p in range(len(PLAN[name][1])):
                    split_ahead(make_hi, act, name, p, i)
                    drain(p, i)
            iterations(act, name, body)

        def nothing(p, i):
            pass

        def transition(t):
            if t > 0:
                act.wait_ge(post_sum, t)
                fn(root[:], X[0][:, 0:T], ACT.Sqrt, scale=1.0 / D_MODEL, bias=eps_col).then_inc(post_root, 1)
            if t < upto:
                with act.Fori(0, KT) as m:
                    act.wait_ge(h_ready, m + (KT * t + 1))
                    fn(x_hi[:, m, :], h[:, m, :], ACT.Identity, scale=pre_w(t, m)).then_inc(x_hi_made, 1)
                    fn(mo[:, m, :], h[:, m, :], ACT.Square).then_inc(h_squared, 1)
                act.wait_ge(pre_sum, t + 1)
                fn(root[:], X[1][:, 0:T], ACT.Sqrt, scale=1.0 / D_MODEL, bias=eps_col).then_inc(pre_root, 1)

        for u in range(3):
            make_hi(act, u, 0, 0)
        act.wait_ge(params_ready, 1)
        link(fn(derived[:, 34:42], par("lam", 0, 8), ACT.Abs))
        fn(derived[:, 42:50], derived[:, 34:42], ACT.Exp, scale=-1.0).then_inc(lam_exp, 1)
        for k in range(KT):
            act.wait_ge(h_turned, k + 1)
            fn(h[:, k, :], X[2 + k % 2][:, 0:T], ACT.Copy).then_inc(h_ready, 1)
        transition(0)

        stream("wag", nothing)
        act.wait_ge(lora_in, 1)
        link(fn(lora[0:64, 0, :], lora[0:64, 0, :], ACT.Tanh))
        fn(lora[:, 1, :], lora[:, 1, :], ACT.Sigmoid).then_inc(lora_made, 1)
        stream("rkv", nothing)

        def lru(p, i):
            if p == 0:
                return
            act.wait_ge(gates_summed, i + 1)
            for m in range(2):
                fn(rg[:, m, :], X[m][:, 0:T], ACT.Sigmoid, bias=par("ga_b", i * 2 + m))
                last = fn(ig[:, m, :], X[2 + m][:, 0:T], ACT.Sigmoid, bias=par("gx_b", i * 2 + m))
            last.then_inc(gates_made, 1)
            act.wait_ge(gates_made, i + 1)
            for m in range(2):
                fn(aa[:, m, :], rg[:, m, :], ACT.Exp, scale=der("neg8sp", i * 2 + m))
                last = fn(th[:, m, :], rg[:, m, :], ACT.Tanh, scale=der("pos8sp", i * 2 + m))
            last.then_inc(decays_made, 1)
            act.wait_ge(lru_root_in, i + 1)
            fn(th[:], th[:], ACT.Sqrt).then_inc(lru_root, 1)
            wait_drained(act, "lru", 1, i)
            fn(ly[:], ly[:], ACT.Gelu_apprx_tanh).then_inc(lru_gelu, 1)
            act.wait_ge(lru_made, i + 1)
            fn(y_hi[:, ds(i * 2, 2), :], lx[:], ACT.Copy).then_inc(y_hi_made, 1)

        stream("lru", lru)
        rwkv_act(act, fn)

        def project(t, from_mo):
            def drain(p, i):
                name = SUBLAYERS[t][3]
                tile = i * 4 + 2 * p
                act.wait_ge(added, i * 4 + (20 * t + 2 * p + 2))
                if from_mo:
                    wait_drained(act, name, p, i)
                    fn(sq[:, p], mo[:, ds(tile, 2), :], ACT.Square).then_inc(squared, 1)
                else:
                    wait_panel(act, name, p, i)
                    fn(sq[:, p], bank(FIRST[name] + p), ACT.Square).then_inc(squared, 1)
                    fn(mo[:, ds(tile, 2), :], bank(FIRST[name] + p), ACT.Copy).then_inc(drained[(FIRST[name] + p) % 2], 1)
            return drain

        stream("out0", project(0, False))
        transition(1)

        def ffn(layer):
            for n in range(3):
                name = f"gv{layer}_{n}"

                def gate_value(p, i, name=name):
                    c = GV_COUNT[name]
                    if p == 0:
                        act.wait_ge(conv_made, i + (c + 1))
                        fn(gelu[:], conv[:], ACT.Gelu_apprx_tanh).then_inc(gelu_made, 1)
                    else:
                        act.wait_ge(prod_made, i + (c + 1))
                        fn(y_hi[:, ds(i * 2, 2), :], prod[:], ACT.Copy).then_inc(y_hi_made, 1)

                stream(name, gate_value)

                def first_sum(p, i, name=f"dn{layer}_0"):
                    wait_panel(act, name, p, i)
                    fn(mo[:, ds(i * 4 + 2 * p, 2), :], bank(FIRST[name] + p), ACT.Copy).then_inc(
                        drained[(FIRST[name] + p) % 2], 1)

                stream(f"dn{layer}_{n}", (first_sum, nothing, project(2 * layer + 1, True))[n])
            transition(2 * layer + 2)

        if upto >= 2:
            ffn(0)
        if upto >= 3:
            stream("gla_qkv", nothing)
            stream("gla_g", nothing)
            gla_act(act, fn)
            stream("out1", project(2, False))
            transition(3)
        if upto >= 4:
            ffn(1)
        for n in range(8):
            b, g = divmod(n, 4)
            act.wait_ge(out_turned, n + 1)
            fn(out_tok[:, b, g * 512:(g + 1) * 512], X[g][:], ACT.Copy).then_inc(out_copied, 1)

    @block.gpsimd
    def _(pool):
        link = Chain(pool, pool_chain)
        for src, group, row, count in param_pieces(A):
            pool.dma_start(par_rows[row:row + count, group, :], src).then_inc(params_landed, 16)
        pool.memset(gate_w[:], 0.0).then_inc(gatew_zeroed, 1)
        pool.wait_ge(gatew_zeroed, 1)

        def gate_weights(i):
            for n, name in enumerate(("lru_gate_a_w", "lru_gate_x_w")):
                for e in range(2):
                    src = A[name][0].rearrange("(m e) a b -> a m e b", e=2)[:, ds(i * 2, 2), e, :]
                    pool.dma_start(gate_w[64 * e:64 * e + 64, 2 * n:2 * n + 2, 64 * e:64 * e + 64],
                                   src).then_inc(gatew_landed, 16)

        gate_weights(0)
        def a_squared(i):
            pool.wait_ge(decays_made, i + 1)
            pool.tensor_tensor(rg[:], aa[:], aa[:], ALU.mult).then_inc(a2_made, 1)

        with pool.Fori(0, 3) as i:
            pool.wait_ge(gates_summed, i + 1)
            gate_weights(i + 1)
            a_squared(i)
        a_squared(3)
        rwkv_pool(pool)

        def sum_squares(t):
            pool.memset(acc[:], 0.0).then_inc(added, 4)

            def body(i):
                for p in range(2):
                    pool.wait_ge(squared, i * 2 + (8 * t + p + 1))
                    for m in range(2):
                        c = 20 * t + 2 * p + m + 4
                        pool.wait_ge(added, i * 4 + c)
                        pool.tensor_tensor(acc[:], acc[:], sq[:, p, m, :], ALU.add).then_inc(added, 1)
            with pool.Fori(0, 4) as i:
                body(i)

        sum_squares(0)
        if upto >= 2:
            pool.wait_ge(unit_used, UNITS * FIRST["dn0_2"])
            sum_squares(1)
        if upto >= 3:
            gla_pool(pool)
            sum_squares(2)
        if upto >= 4:
            pool.wait_ge(unit_used, UNITS * FIRST["dn1_2"])
            sum_squares(3)

    @block.vector
    def _(dve):
        link = Chain(dve, dve_chain)
        tt, stt, ts = nc.vector.tensor_tensor, nc.vector.scalar_tensor_tensor, nc.vector.tensor_scalar

        def stream(name, drain, steps=0):
            iters, panels = PLAN[name]

            def body(i):
                for p in range(len(panels)):
                    split_ahead(make_lo, dve, name, p, i)
                    drain(p, i)
            if iters == 1:
                body(0)
                return
            end = iters - 1 if name == LAST_PHASE else iters
            with link.loop(end, steps) as i:
                body(i)
            if name == LAST_PHASE:
                body(iters - 1)

        def scaled(dst, name, p, i):
            wait_panel(dve, name, p, i)
            n = FIRST[name] + p
            tt(dst, bank(n), wide(rpre[:]), ALU.mult).then_inc(drained[n % 2], 1)
            wait_drained(dve, name, p, i)

        def split_y(tiles, source, count):
            dve.wait_ge(y_hi_made, count)
            tt(y_lo[:, tiles, :], source, y_hi[:, tiles, :].bitcast(F32), ALU.subtract).then_inc(y_lo_made, 1)

        def transition(t):
            if t > 0:
                dve.wait_ge(post_root, t)
                link(nc.vector.reciprocal(rpost[:], root[:]))

                def residual(m):
                    link(tt(mo[:, m, :], mo[:, m, :], rpost[:], ALU.mult))
                    stt(h[:, m, :], mo[:, m, :], post_w(t - 1, m), h[:, m, :], ALU.mult, ALU.add).then_inc(h_ready, 1)
            if t < upto:
                def low(m):
                    dve.wait_ge(x_hi_made, m + (KT * t + 1))
                    stt(x_lo[:, m, :], h[:, m, :], pre_w(t, m), x_hi[:, m, :].bitcast(F32), ALU.mult,
                        ALU.subtract).then_inc(x_lo_made, 1)
            if t == 0:
                with dve.Fori(0, KT) as m:
                    low(m)
            elif t < upto:
                residual(0)
                with link.loop(KT - 1, 1, 1) as m:
                    residual(m)
                    low(m - 1)
                low(KT - 1)
            else:
                with link.loop(KT, 1) as m:
                    residual(m)
            if t < upto:
                dve.wait_ge(pre_root, t + 1)
                link(nc.vector.reciprocal(rpre[:], root[:]))

        for u in range(3):
            make_lo(dve, u, 0, 0)
        nc.vector.memset(eps_col, NORM_EPS)
        nc.vector.memset(gn_eps_col, GN_EPS)
        dve.wait_ge(par_turned, 1)
        nc.vector.tensor_copy(params[:, 0:512], X[0][:])
        nc.vector.tensor_copy(params[:, 512:N_COLS], X[1][:, 0:N_COLS - 512]).then_inc(params_ready, 1)
        dve.wait_ge(params_ready, 1)
        link(ts(der("one_minus_mu", 0, 26), par("mu", 0, 26), -1.0, 1.0, ALU.mult, ALU.add))
        link(ts(der("one_minus_ka", 0, 8), par("k_a", 0, 8), -1.0, 1.0, ALU.mult, ALU.add))
        dve.wait_ge(lam_exp, 1)
        x_c, z_c, z2_c, s_c, den_c = (rpre[:, 8 * k:8 * k + 8] for k in range(5))
        link(ts(den_c, derived[:, 42:50], 2.0, None, ALU.add))
        link(nc.vector.reciprocal(den_c, den_c))
        link(tt(z_c, derived[:, 42:50], den_c, ALU.mult))
        link(tt(z2_c, z_c, z_c, ALU.mult))
        link(ts(s_c, z2_c, 1.0 / 15, None, ALU.mult))
        for k in (13, 11, 9, 7, 5, 3):
            link(stt(s_c, s_c, 1.0 / k, z2_c, ALU.add, ALU.mult))
        link(stt(s_c, s_c, 1.0, z_c, ALU.add, ALU.mult))
        link(ts(x_c, par("lam", 0, 8), -1.0, 0.0, ALU.mult, ALU.max))
        link(stt(s_c, s_c, 2.0, x_c, ALU.mult, ALU.add))
        link(ts(der("neg8sp", 0, 8), s_c, -8.0, None, ALU.mult))
        link(ts(der("pos8sp", 0, 8), s_c, 8.0, None, ALU.mult))
        transition(0)

        link(nc.vector.memset(u_in[:, :, 0:1], 0.0))

        def shifted(name, dst, mu_of):
            def drain(p, i):
                scaled(u_in[:, :, 1:T + 1], name, p, i)
                for m in range(2):
                    link(ts(dst(p, i, m), u_in[:, m, 1:T + 1], der("one_minus_mu", mu_of(p, i, m)), None, ALU.mult))
                    link(stt(dst(p, i, m), u_in[:, m, 0:T], par("mu", mu_of(p, i, m)), dst(p, i, m), ALU.mult, ALU.add))
            return drain

        stream("wag", shifted("wag", lambda p, i, m: lora[:, m, :], lambda p, i, m: 24 + m))
        dve.sem_inc(lora_in, 1)
        stream("rkv", shifted("rkv", lambda p, i, m: rkv[:, i * 4 + (2 * p + m), :], lambda p, i, m: i * 4 + (2 * p + m)), 8)
        link(nc.vector.memset(lx_in[:, :, 0:3], 0.0))

        def lru(p, i):
            if p == 0:
                scaled(lx_in[:, :, 3:T + 3], "lru", 0, i)
                for m in range(2):
                    def tap(k):
                        return par("lru_cw", i * 2 + (8 * k + m))
                    link(ts(lx[:, m, :], lx_in[:, m, 3:T + 3], tap(3), par("lru_cb", i * 2 + m), ALU.mult, ALU.add))
                    for k in (2, 1, 0):
                        last = stt(lx[:, m, :], lx_in[:, m, k:k + T], tap(k), lx[:, m, :], ALU.mult, ALU.add)
                        if k or not m:
                            link(last)
                last.then_inc(lx_made, 1)
                return
            scaled(ly[:], "lru", 1, i)
            dve.wait_ge(gates_made, i + 1)
            link(tt(ig[:], ig[:], lx[:], ALU.mult))
            dve.wait_ge(a2_made, i + 1)
            stt(th[:], rg[:], 1.0, th[:], ALU.add, ALU.mult).then_inc(lru_root_in, 1)
            dve.wait_ge(lru_root, i + 1)
            link(tt(ig[:], ig[:], th[:], ALU.mult))
            for m in range(2):
                link(nc.vector.tensor_tensor_scan(lx[:, m, :], aa[:, m, :], ig[:, m, :], 0.0, ALU.mult, ALU.add))
            dve.wait_ge(lru_gelu, i + 1)
            tt(lx[:], lx[:], ly[:], ALU.mult).then_inc(lru_made, 1)
            split_y(ds(i * 2, 2), lx[:], i + 1)

        stream("lru", lru, 11)
        rwkv_dve(dve, link, tt, stt, ts, split_y)

        def nothing(p, i):
            pass

        stream("out0", nothing)
        transition(1)

        def ffn(layer):
            link(nc.vector.memset(gate_in[:, :, 0:2], 0.0))
            for n in range(3):
                name = f"gv{layer}_{n}"

                def gate_value(p, i, name=name, n=n):
                    c = GV_COUNT[name]
                    if p == 0:
                        scaled(gate_in[:, :, 2:T + 2], name, 0, i)
                        for m in range(2):
                            f = 2 * FFN_PARTS[n][0] + m

                            def tap(k):
                                return par("ffn_cw", i * 2 + (132 * layer + 44 * k + f))
                            link(ts(conv[:, m, :], gate_in[:, m, 2:T + 2], tap(2), par("ffn_cb", i * 2 + (44 * layer + f)),
                                    ALU.mult, ALU.add))
                            link(stt(conv[:, m, :], gate_in[:, m, 1:T + 1], tap(1), conv[:, m, :], ALU.mult, ALU.add))
                            last = stt(conv[:, m, :], gate_in[:, m, 0:T], tap(0), conv[:, m, :], ALU.mult, ALU.add)
                        last.then_inc(conv_made, 1)
                    else:
                        scaled(val[:], name, 1, i)
                        dve.wait_ge(gelu_made, i + (c + 1))
                        tt(prod[:], val[:], gelu[:], ALU.mult).then_inc(prod_made, 1)
                        y_before = 12 + c + (4 if layer else 0)
                        split_y(ds(i * 2, 2), prod[:], i + (y_before + 1))

                stream(name, gate_value, 4)

                def add_up(p, i, name=f"dn{layer}_{n}"):
                    wait_panel(dve, name, p, i)
                    tiles = mo[:, ds(i * 4 + 2 * p, 2), :]
                    tt(tiles, bank(FIRST[name] + p), tiles, ALU.add).then_inc(drained[(FIRST[name] + p) % 2], 1)

                stream(f"dn{layer}_{n}", (nothing, add_up, add_up)[n])
            transition(2 * layer + 2)

        if upto >= 2:
            ffn(0)
        if upto >= 3:
            dve.wait_ge(gdw_landed, 16)
            gd_pre = par("mix_pre", KT, KT).unsqueeze(2).broadcast_to([P, KT, 16])
            tt(gd_w[:], gd_w[:], gd_pre, ALU.mult).then_inc(gdw_made, 1)
            stream("gla_qkv", lambda p, i: scaled(qkv[:, ds(i * 4 + 2 * p, 2), :], "gla_qkv", p, i))
            stream("gla_g", lambda p, i: scaled(g_all[:, ds(i * 4 + 2 * p, 2), :], "gla_g", p, i))
            gla_dve(dve, link, tt, stt, ts, split_y)
            stream("out1", nothing)
            transition(3)
        if upto >= 4:
            ffn(1)


def flat_rows(ap):
    if len(ap.shape) == 2:
        return ap.rearrange("a (r p) -> (a r) p", p=P)
    if ap.shape[-1] == 64:
        return ap.rearrange("a (r e) c -> (a r) (e c)", e=2)
    return ap.rearrange("a k (r p) -> (a k r) p", p=P)


PARAM_SOURCE = {"mix_pre": "mix_pre_norm", "mix_post": "mix_post_norm", "ffn_pre": "ffn_pre_norm", "ffn_post": "ffn_post_norm",
                "lru_cw": "lru_conv_w", "lru_cb": "lru_conv_b", "ga_b": "lru_gate_a_b", "gx_b": "lru_gate_x_b",
                "lam": "lru_lambda", "mu": "rwkv_shift_mu", "w0": "rwkv_w0", "a0": "rwkv_a0", "k_k": "rwkv_k_k",
                "k_a": "rwkv_k_a", "r_k": "rwkv_r_k", "ln_w": "rwkv_ln_w", "ln_b": "rwkv_ln_b", "gk_b": "gla_gk_b",
                "gla_nw": "gla_norm_w", "ffn_cw": "ffn_conv_w", "ffn_cb": "ffn_conv_b"}


def param_spans():
    for name, rows in PARAM_ROWS:
        done = 0
        while done < rows:
            group, row = divmod(COL[name] + done, P)
            count = min(rows - done, P - row)
            yield name, done, group, row, count
            done += count


N_PARAM_DMAS = len(list(param_spans()))


def param_pieces(A):
    for name, done, group, row, count in param_spans():
        yield flat_rows(A[PARAM_SOURCE[name]])[done:done + count, :], group, row, count


_INS = ['x', 'meta_tokens', 'mix_pre_norm', 'mix_post_norm', 'ffn_pre_norm', 'ffn_post_norm', 'ab_w_in', 'lru_conv_w',
        'lru_conv_b', 'lru_gate_a_w', 'lru_gate_a_b', 'lru_gate_x_w', 'lru_gate_x_b', 'lru_lambda', 'rwkv_shift_mu',
        'rwkv_w0', 'rwkv_w2', 'rwkv_a0', 'rwkv_a2', 'rwkv_g2', 'rwkv_k_k', 'rwkv_k_a', 'rwkv_r_k', 'rwkv_ln_w',
        'rwkv_ln_b', 'ab_w_out', 'gla_w_in', 'gla_gk_up', 'gla_gk_b', 'gla_norm_w', 'gla_w_out', 'ffn_w_gate',
        'ffn_w_val', 'ffn_conv_w', 'ffn_conv_b', 'ffn_w_down']


def kernel(**inputs):
    import concourse.bacc as bacc
    from concourse.bass_utils import run_bass_kernel_spmd

    nc = bacc.Bacc("TRN2", target_bir_lowering=False, num_devices=1)
    arrays = {name: np.ascontiguousarray(inputs[name]) for name in _INS}
    arrays.update(zip(("const_rwkv", "const_gla", "const_trunk"), constants()))
    A = {name: nc.dram_tensor(name, a.shape, mybir.dt.from_np(a.dtype), kind="ExternalInput").ap()
         for name, a in arrays.items()}
    A["out"] = nc.dram_tensor("out", (1, SEQ, D_MODEL), F32, kind="ExternalOutput").ap()
    trunk_kernel(nc, A)
    r = run_bass_kernel_spmd(nc, [arrays], core_ids=[0])
    return r.results[0]["out"]
```

```python
import concourse.bass as bass
from concourse import mybir
from contextlib import ExitStack, contextmanager
import numpy as np

F32 = mybir.dt.float32
F32R = mybir.dt.float32r
ALU = mybir.AluOpType
ACT = mybir.ActivationFunctionType
ds = bass.ds

P = 128
D_MODEL = 2048
KT = D_MODEL // P
N_META = 16
SEQ = 256
T = N_META + SEQ
PANEL = 256
UNIT_KT = 4
UNITS = 4
RAW_SLOTS = 8
SPLIT_SLOTS = 4
LRU_WIDTH = 1024
RW = 1024
GLA_KW = 1024
GLA_VW = 2048
FFN_PARTS = ((0, 8), (8, 8), (16, 6))
NORM_EPS = 1e-6
GN_EPS = 64e-5
DECAY = float(np.exp(-0.5))
CH = 64
LEVELS = (2, 4, 8, 16, 32)
TAIL = T - 2 * P
GLA_LEVELS = (1, 2, 4, 8, 16, 32, 64)
GLA_DK = 256
GLA_DV = 512

PARAM_ROWS = [("mix_pre", 32), ("mix_post", 32), ("ffn_pre", 32), ("ffn_post", 32),
              ("lru_cw", 32), ("lru_cb", 8), ("ga_b", 8), ("gx_b", 8), ("lam", 8),
              ("mu", 26), ("w0", 8), ("a0", 8), ("k_k", 8), ("k_a", 8), ("r_k", 8), ("ln_w", 8), ("ln_b", 8),
              ("gk_b", 8), ("gla_nw", 4), ("ffn_cw", 264), ("ffn_cb", 88)]
COL, _c = {}, 0
for _n, _r in PARAM_ROWS:
    COL[_n] = _c
    _c += _r
N_COLS = _c
PT_GROUPS = -(-N_COLS // P)
DCOL = {"one_minus_mu": 0, "one_minus_ka": 26, "neg8sp": 34, "pos8sp": 42}
N_DCOLS = 50


def constants():
    t = np.arange(P)
    row, col = t[:, None], t[None, :]
    same = (row // CH) == (col // CH)
    strict_up, incl_up = (row < col) & same, (row <= col) & same
    parts = [strict_up, incl_up, strict_up, -1.0 * incl_up, (row > col) & same]
    pair_low = (row // 2 == col // 2) & (row > col)
    parts += [pair_low, pair_low.T]
    for size in LEVELS:
        parts.append((row // (2 * size) == col // (2 * size)) & (row // size > col // size))
    chunk = np.stack([t // CH == 0, t // CH == 1], 1)
    restart = np.ones((P, T))
    restart[:, ::CH] = 0.0
    parts += [chunk, -1.0 * chunk, restart]
    rwkv = np.concatenate([np.asarray(p, np.float32) for p in parts], 1)
    scale = GLA_DK ** -0.5
    gla = [scale * (row == col)]
    for size in GLA_LEVELS:
        gla.append(scale * ((row // (2 * size) == col // (2 * size)) & (row // size < col // size)))
    gla = np.concatenate([np.asarray(p, np.float32) for p in gla], 1)
    head = (row // 64) == (col // 64)
    trunk = np.concatenate([np.asarray(p, np.float32) for p in (row == col, np.ones((P, P)), head)], 1)
    return rwkv, gla, trunk


def phases(upto):
    out = [("wag", 1, [("ab_w_in", 2 * LRU_WIDTH + 3 * RW, 0, 0, 4)]),
           ("rkv", 6, [("ab_w_in", 2 * LRU_WIDTH + PANEL * k, 2 * PANEL, 0, 4) for k in range(2)]),
           ("lru", 4, [("ab_w_in", 0, PANEL, 0, 4), ("ab_w_in", LRU_WIDTH, PANEL, 0, 4)]),
           ("out0", 4, [("ab_w_out", PANEL * k, 2 * PANEL, 0, 4) for k in range(2)])]

    def ffn(layer):
        for n, (first, count) in enumerate(FFN_PARTS):
            out.append((f"gv{layer}_{n}", count, [(f"{w}{layer}", PANEL * first, PANEL, 0, 4) for w in ("gate", "val")]))
            out.append((f"dn{layer}_{n}", 4, [(f"down{layer}", PANEL * k, 2 * PANEL, PANEL * first, count // 2)
                                              for k in range(2)]))
    if upto >= 2:
        ffn(0)
    if upto >= 3:
        qkv = 2 * GLA_KW + GLA_VW
        out.append(("gla_qk", 4, [("gla_w_in", PANEL * k, 2 * PANEL, 0, 4) for k in range(2)]))
        out.append(("gla_vg", 4, [("gla_w_in", c + PANEL * k, 2 * PANEL, 0, 4) for c in (2 * GLA_KW, qkv) for k in range(2)]))
        out.append(("out1", 4, [("gla_w_out", PANEL * k, 2 * PANEL, 0, 4) for k in range(2)]))
    if upto >= 4:
        ffn(1)
    return out


class Chain:

    def __init__(self, engine, sem):
        self.engine, self.sem, self.base, self.here, self.i, self.per = engine, sem, 0, 0, 0, 0

    def __call__(self, ins):
        ins.then_inc(self.sem, 1)
        self.here += 1
        self.engine.wait_ge(self.sem, self.i * self.per + (self.base + self.here))

    @contextmanager
    def loop(self, count, per, start=0):
        assert self.here == 0 or self.per == 0
        self.base, self.here, self.per = self.base + self.here - start * per, 0, per
        with self.engine.Fori(start, start + count) as i:
            self.i = i
            yield i
        assert self.here == per, (self.here, per)
        self.base, self.here, self.i, self.per = self.base + (start + count) * per, 0, 0, 0


def trunk_kernel(nc, A, upto=4):
    ctx = ExitStack()
    with ctx:
        build(nc, ctx, A, upto)


def build(nc, ctx, A, upto):
    def sb(name, shape, dt=F32):
        return ctx.enter_context(nc.sbuf_tensor(name, shape, dt))

    def at(name, shape, host, offset, dt=F32):
        start, stop = host.manual_base
        size = int(np.prod(shape[1:])) * 4
        assert offset % 32 == 0 and start + offset + size <= stop, (name, offset, size, stop - start)
        return nc.alloc_sbuf_tensor_at(name, shape, dt, offset=start + offset)

    class Region:
        def __init__(self, name, shape, dt=F32):
            size = -(-int(np.prod(shape[1:])) * 4 // 32) * 32
            start = Region.top
            Region.top += size
            assert Region.top <= nc.sbuf_usable_end, (name, Region.top)
            self.manual_base = (start, start + size)
            self.t = nc.alloc_sbuf_tensor_at(name, shape, dt, offset=start)

        def __getitem__(self, k):
            return self.t[k]

    Region.top = -(-nc.sbuf_base // 32) * 32
    raw = Region("raw", [P, RAW_SLOTS, UNIT_KT, PANEL])
    w_hi = Region("w_hi", [P, SPLIT_SLOTS, UNIT_KT, PANEL], F32R)
    w_lo = Region("w_lo", [P, SPLIT_SLOTS, UNIT_KT, PANEL], F32R)
    h = Region("h", [P, KT, T])
    xs = Region("xs", [P, 2, KT, T])
    x_hi = at("x_hi", [P, KT, T], xs, 0, F32R)
    x_lo = at("x_lo", [P, KT, T], xs, KT * T * 4, F32R)
    y_hi = Region("y_hi", [P, KT, T], F32R)
    y_lo = Region("y_lo", [P, KT, T], F32R)
    mo = Region("mo", [P, KT, T])
    r1 = Region("r1", [P, 32, T])
    trunk_c = Region("trunk_c", [P, 3, P])
    params = Region("params", [P, PT_GROUPS * P])
    derived = Region("derived", [P, N_DCOLS + 5])
    rpre = Region("rpre", [P, T])
    small = Region("small", [P, 528])
    ident, ones, head_ones = trunk_c[:, 0, :], trunk_c[:, 1, :], trunk_c[:, 2, :]
    eps_col, gn_eps_col = derived[:, N_DCOLS:N_DCOLS + 1], derived[:, N_DCOLS + 1:N_DCOLS + 2]

    def par(name, i, count=1):
        return params[:, ds(COL[name] + i, count)]

    def der(name, i, count=1):
        return derived[:, ds(DCOL[name] + i, count)]

    TB = T * 4
    x_tok = at("x_tok", [P, 2, D_MODEL], r1, 0)
    meta_tok = at("meta_tok", [N_META, D_MODEL], r1, 16384)
    par_rows = at("par_rows", [P, PT_GROUPS, P], r1, 24576)
    h_sum = at("h_sum", [P, T], small, 0)
    acc = at("acc", [P, T], r1, 0)
    sq = at("sq", [P, 2, 2, T], r1, TB)
    root = at("root", [P, T], r1, 5 * TB)
    rpost = at("rpost", [P, T], r1, 6 * TB)
    gate_in = at("gate_in", [P, 2, T + 2], r1, 7 * TB + 0)
    conv = at("conv", [P, 2, T], r1, 10 * TB)
    gelu = at("gelu", [P, 2, T], r1, 12 * TB)
    val = at("val", [P, 2, T], r1, 14 * TB)
    prod = at("prod", [P, 2, T], r1, 16 * TB)
    rkv = at("rkv", [P, 24, T], r1, 0)
    lora = at("lora", [P, 2, T], r1, 24 * TB)
    gate_w = at("gate_w", [P, 4, P], r1, 28288)
    u_in = at("u_in", [P, 2, T + 1], mo, 0)
    lx_in = at("lx_in", [P, 2, T + 3], mo, 0)
    lx = at("lx", [P, 2, T], mo, 2208)
    rg = at("rg", [P, 2, T], mo, 4384)
    ig = at("ig", [P, 2, T], mo, 6560)
    aa = at("aa", [P, 2, T], mo, 8736)
    th = at("th", [P, 2, T], mo, 10912)
    ly = at("ly", [P, 2, T], mo, 13088)

    class PairBuffers:

        def __init__(self, g):
            def slot(name, n, count=1, width=T):
                host, off = (mo, n * TB) if g == 0 else ((y_hi, (8 + n) * TB) if n < 8 else (y_lo, n * TB))
                return at(f"{name}_{g}", [P, count, width] if count > 1 else [P, width], host, off)

            names = ("kk", "inv", "dk", "ag", "gg", "cum", "e_neg", "e_pos", "k2", "rk")
            (self.kk, self.inv, self.dk, self.ag, self.gg, self.cum, self.e_neg, self.e_pos, self.k2,
             self.rk) = (slot(name, n) for n, name in enumerate(names))
            self.ar = slot("ar", 10, 2)
            self.beta, self.kappa = slot("beta", 12), slot("kappa", 13)
            self.beta_end, self.kappa_end = slot("beta_end", 14, 1, 2 * P), slot("kappa_end", 15, 1, 2 * P)

            def place(name, shape, spot0, spot1):
                host, off = (spot0, spot1)[g]
                return at(f"{name}_{g}", shape, host, off)

            self.A4 = place("A4", [P, 2, 2, 2 * P], (xs, 7264), (w_hi, 0))
            self.B4 = place("B4", [P, 2, 2, 2 * P], (xs, 11360), (w_hi, 4096))
            self.M4 = place("M4", [P, 4, P], (xs, 15456), (w_hi, 8192))
            self.Z4 = place("Z4", [P, 4, P], (xs, 17504), (w_hi, 10240))
            self.W4 = place("W4", [P, 4, P], (xs, 19552), (w_hi, 12288))
            self.T4 = place("T4", [P, 4, P], (xs, 21600), (w_lo, 0))
            self.F4 = place("F4", [P, 4, P], (xs, 23648), (w_lo, 2048))
            self.XX = place("XX", [P, 2, 2, 2, 64], (xs, 25696), (w_lo, 4096))
            self.BX = place("BX", [P, 2, 2, 2, 64], (xs, 27744), (w_lo, 6144))
            self.KX = place("KX", [P, 2, 2, 2, 64], (xs, 29792), (w_lo, 8192))
            self.tXX = place("tXX", [TAIL, 2, 2, 64], (xs, 31840), (w_hi, 14336))
            self.rq = place("rq", [P, T], (xs, 32864), (w_lo, 10240))
            self.gbd = place("gbd", [P, 4, P], (xs, 21600), (w_lo, 0))
            self.dci = place("dci", [P, 4, 64], (xs, 23648), (w_lo, 2048))
            self.v_tok = place("v_tok", [P, 2, P], (small, 0), (w_hi, 15360))
            self.v_loc = place("v_loc", [P, T], (small, 1024), (w_lo, 11328))
            self.state = place("state", [P, 5, P], (r1, 29952), (w_lo, 12416))
            self.tA = place("tA", [TAIL, 2, 2, TAIL], (r1, 28288), (w_lo, 14976))
            self.tB = place("tB", [TAIL, 2, 2, TAIL], (r1, 28544), (w_lo, 15232))
            self.tM, self.tZ, self.tW, self.tT, self.tF = (
                place(n, [TAIL, 2, TAIL], (r1, 28800 + 128 * k), (w_lo, 15488 + 128 * k))
                for k, n in enumerate(("tM", "tZ", "tW", "tT", "tF")))
            self.tV = place("tV", [TAIL, P], (r1, 29440), (xs, 33952))
            self.pair_w = at(f"pair_w_{g}", [P, 2, P], r1, 32512 + 1024 * g)
            self.X = X if g == 0 else [main_ps[n // 2][:, n % 2, :] for n in range(4)]

    rw_c = at("rw_c", [P, 1812], xs, 0)
    MASK = {"A": 0, "B": 256, "M": 512, "pair": 640, "pairT": 768, "levels": 896, "chunk": 1536, "nchunk": 1538,
            "restart": 1540}

    def mask(name, n=P, rows=P):
        return rw_c[0:rows, MASK[name]:MASK[name] + n]

    qk = at("qk", [P, 16, T], r1, 0)
    gd_w = at("gd_w", [P, KT, 16], small, 0)
    gd_t = at("gd_t", [16, T], small, 1024)
    o_gated = at("o_gated", [P, KT, T], mo, 0)
    gl_c = at("gl_c", [P, 8, P], y_hi, 0)
    gk_w = at("gk_w", [16, GLA_DK], y_hi, 4096)
    k_loc = at("k_loc", [P, 2, T], y_hi, 5120)
    v_in = at("v_in", [P, 4, T], y_hi, 7296)
    gk = at("gk", [P, 2, T], y_hi, 11648)
    soft = at("soft", [P, 2, T], y_hi, 13824)
    at1 = at("at1", [P, P + TAIL], y_hi, 16000)
    at2 = at("at2", [TAIL, TAIL], y_hi, 16576)
    part2 = at("part2", [TAIL, TAIL], y_hi, 16640)
    v_rows = at("v_rows", [P, 3, GLA_DV], y_lo, 0)
    at0 = at("at0", [P, T], y_lo, 6144)
    part = at("part", [P, 2, P], y_lo, 7232)
    gsq = at("gsq", [P, 4, T], y_lo, 8256)
    gr = at("gr", [P, T], y_lo, 12608)
    logits = at("logits", [P, 2, T], y_lo, 13696)
    g_loc = at("g_loc", [P, 4, T], r1, 17408)
    o_all = at("o_all", [P, 4, T], r1, 21760)
    diffs = [at(f"diff{n}", [P, 2, T], r1, 26112 + 2176 * n) for n in range(2)]
    levs = [at(f"lev{n}", [P, 2, T], r1, 30464 + 2176 * n) for n in range(2)]
    out_tok = at("out_tok", [P, 2, D_MODEL], xs, 0)

    main_ps = [ctx.enter_context(nc.psum_tensor(f"main{n}", [P, 2, 512], F32)) for n in range(2)]
    X = [ctx.enter_context(nc.psum_tensor(f"aux{n}", [P, 512], F32)) for n in range(4)]

    plan, FIRST, n = phases(upto), {}, 0
    PLAN = {name: (iters, panels) for name, iters, panels in plan}
    for name, iters, panels in plan:
        FIRST[name] = n
        n += iters * len(panels)
    TOTAL_UNITS = UNITS * n
    LAST_PHASE = plan[-1][0]
    views = {}
    for name in ("ab_w_in", "ab_w_out", "gla_w_in", "gla_w_out"):
        views[name] = A[name].rearrange("l (k p) n -> p (l k) n", p=P)
    for layer in range(2):
        for short, full in (("gate", "ffn_w_gate"), ("val", "ffn_w_val"), ("down", "ffn_w_down")):
            views[f"{short}{layer}"] = A[full][layer].rearrange("(k p) n -> p k n", p=P)

    def sem(name):
        return ctx.enter_context(nc.semaphore(name))

    def sems(names):
        return [sem(n) for n in names.split()]

    raw_landed = [sem(f"raw_landed{s}") for s in range(RAW_SLOTS)]
    drained = [sem("drained0"), sem("drained1")]
    hi_made, lo_made, unit_used = sems("hi_made lo_made unit_used")
    act_chain, dve_chain = sems("act_chain dve_chain")
    inputs_landed, trunk_landed, rwc_landed = sems("inputs_landed trunk_landed rwc_landed")
    params_landed = [sem(f"params_landed{n}") for n in range(3)]
    par_turned, params_ready, lam_exp = sems("par_turned params_ready lam_exp")
    h_turned, h_ready, x_hi_made, x_lo_made, h_squared, h_added = sems(
        "h_turned h_ready x_hi_made x_lo_made h_squared h_added")
    pre_sum, pre_root, squared, added, post_sum, post_root, normed = sems(
        "pre_sum pre_root squared added post_sum post_root normed")
    conv_made, gelu_made, prod_made, y_hi_made, y_lo_made = sems("conv_made gelu_made prod_made y_hi_made y_lo_made")
    gatew_landed, gates_summed, gates_made, lx_made, gatew_zeroed = sems(
        "gatew_landed gates_summed gates_made lx_made gatew_zeroed")
    lru_root_in, lru_root, decays_made, a2_made, lru_gelu, lru_made = sems(
        "lru_root_in lru_root decays_made a2_made lru_gelu lru_made")
    lora_in, lora_made = sems("lora_in lora_made")
    out_turned, out_copied, out_landed = sems("out_turned out_copied out_landed")

    def bank(n, start=0):
        return main_ps[n % 2][:, :, start:T]

    def wide(ap, n=2):
        return ap.unsqueeze(1).broadcast_to([ap.shape[0], n, ap.shape[1]])

    Y_BEFORE, Y_COUNT, y = {}, {}, 0
    for name, add in [("out0", 8)] + [(f"dn0_{n}", FFN_PARTS[n][1]) for n in range(3)] + [("out1", 8)] + [
            (f"dn1_{n}", FFN_PARTS[n][1]) for n in range(3)]:
        Y_BEFORE[name] = y
        y += add
        Y_COUNT[name] = y
    GV_COUNT = {"gv0_0": 0, "gv0_1": 8, "gv0_2": 16, "gv1_0": 22, "gv1_1": 30, "gv1_2": 38}
    SUBLAYERS = [("mix_pre", "mix_post", 0, "out0"), ("ffn_pre", "ffn_post", 0, "dn0_2"),
                 ("mix_pre", "mix_post", 1, "out1"), ("ffn_pre", "ffn_post", 1, "dn1_2")][:upto]

    LATE, CONV_LATE = (N_META, N_META - 2) if upto == 4 else (0, 0)
    FROM_IN = (0, 0, 0, CONV_LATE, 0)
    FROM_OUT = (0, 0, CONV_LATE, LATE, 0)

    def first_token(name, p=0):
        if name == "out1" or (name.startswith("gv1") and p == 0):
            return CONV_LATE
        return LATE if name.startswith(("gv1", "dn1")) else 0

    def pre_w(s, m):
        return par(SUBLAYERS[s][0], m + KT * SUBLAYERS[s][2])

    def post_w(s, m):
        return par(SUBLAYERS[s][1], m + KT * SUBLAYERS[s][2])

    PEELED = ("lru", LAST_PHASE)

    FRESH = {"wag": 0, "gv0_0": 1, "gla_qk": 2, "gv1_0": 3}

    def iterations(loop, name, body, peel=False):
        iters, _ = PLAN[name]
        start = int(peel or iters == 1)
        stop = iters - 1 if name in PEELED else iters
        if start:
            body(0)
        if stop > start:
            with loop(start, stop) as i:
                body(i)
        if name in PEELED:
            body(iters - 1)

    def wait_panel(engine, name, p, i):
        per = len(PLAN[name][1])
        engine.wait_ge(unit_used, i * (per * UNITS) + UNITS * (FIRST[name] + p + 1))

    def wait_drained(engine, name, p, i):
        n = FIRST[name] + p
        per = len(PLAN[name][1])
        engine.wait_ge(drained[n % 2], i * (max(per, 2) // 2) + (n // 2 + 1))

    (lora_summed, lora_read, kq_made, kk_summed, kk_root, cum_made, lag_made, e_neg_made, exps_made, rk_made,
     k2_scaled, k2_made, rho_made, bonus_summed, bonus_read, v_loc_made, vt_turned, feats_made, rows_turned, rows_read_act,
     rows_read_dve, gram_made, gram_read, gram2_made, gram2_read, nv_summed, xx_made, moff_made, zw_made, t_summed,
     t_copied, zw_summed, wx_summed, wx_made, rq_summed, rq_made, g_summed, gbd_made, state_summed, state_made,
     y_summed, y_copied, mean_summed, centred, ysq_made, var_summed, gn_root, pair_out) = sems(
        "lora_summed lora_read kq_made kk_summed kk_root cum_made lag_made e_neg_made exps_made rk_made "
        "k2_scaled k2_made rho_made bonus_summed bonus_read v_loc_made vt_turned feats_made rows_turned rows_read_act "
        "rows_read_dve gram_made gram_read gram2_made gram2_read nv_summed xx_made moff_made zw_made t_summed "
        "t_copied zw_summed wx_summed wx_made rq_summed rq_made g_summed gbd_made state_summed state_made "
        "y_summed y_copied mean_summed centred ysq_made var_summed gn_root pair_out")
    pairw_landed = [sem("pairw_landed0"), sem("pairw_landed1")]
    PAIRS = RW // P
    NL = len(LEVELS)
    TAIL_LEVELS = sum(2 * size <= TAIL for size in LEVELS)
    HEAD = (slice(0, 64), slice(64, P))
    BLK = (slice(0, P), slice(P, 2 * P))
    END = slice(2 * P, T)
    BUF = [PairBuffers(g) for g in range(2)]
    BOTH = ((0, BUF[0]), (1, BUF[1]))

    def nth(i, g, per=1, n=0):
        return i * (2 * per) + (2 * n + g + 1)

    def cols(q, n):
        return slice(q * n, (q + 1) * n)

    def by2(ap):
        return ap.rearrange("p (a t) -> p a t", a=2)

    def by4(ap):
        return ap.rearrange("p (a t) -> p a t", a=4)

    def rwkv_pe(pe, mm, turn):
        pe.wait_ge(lora_made, 1)
        pe.wait_ge(y_lo_made, LRU_WIDTH // PANEL)

        def keep_warm(bank, n):
            for _ in range(n):
                mm(bank[:, T:512], ones, trunk_c[:].rearrange("p a b -> p (a b)")[:, 0:512 - T])

        with pe.Fori(0, PAIRS // 2) as i:
            for g, B in BOTH:
                pe.wait_ge(pair_out, nth(i, g))
                pe.wait_ge(pairw_landed[g], i * 48 + 48)
                mm(B.X[0][:, 0:T], B.pair_w[0:64, 0, :], lora[0:64, 0, :])
                mm(B.X[1][:, 0:T], B.pair_w[64:P, 0, :], lora[64:P, 0, :])
                mm(B.X[2][:, 0:T], B.pair_w[:, 1, :], lora[:, 1, :]).then_inc(lora_summed, 1)
                pe.wait_ge(kq_made, nth(i, g))
                mm(B.X[3][:, 0:T], head_ones, B.inv[:]).then_inc(kk_summed, 1)
            for g, B in BOTH:
                pe.wait_ge(v_loc_made, nth(i, g))
                pe.wait_ge(lora_read, nth(i, g))
                for b in range(2):
                    turn(B.X[1][:, cols(b, P)], B.v_loc[:, BLK[b]])
                turn(B.X[1][0:TAIL, 256:384], B.v_loc[:, END]).then_inc(vt_turned, 1)
            keep_warm(X[2], 18)
            for g, B in BOTH:
                pe.wait_ge(rk_made, nth(i, g))
                mm(B.X[0][:, 0:T], head_ones, B.rk[:]).then_inc(bonus_summed, 1)
            keep_warm(X[2], 8)
            for g, B in BOTH:
                pe.wait_ge(feats_made, nth(i, g))
                for b in range(2):
                    turn(B.X[2][:, cols(b, P)], B.ar[:, 0, BLK[b]])
                turn(B.X[2][0:TAIL, 256:384], B.ar[:, 0, END])
                for b in range(2):
                    turn(B.X[3][:, cols(b, P)], B.beta_end[:, BLK[b]])
                    ins = turn(B.X[3][:, cols(2 + b, P)], B.kappa_end[:, BLK[b]])
                ins.then_inc(rows_turned, 1)
            for g, B in BOTH:
                pe.wait_ge(rows_read_act, nth(i, g))
                pe.wait_ge(rows_read_dve, nth(i, g))
                pe.wait_ge(bonus_read, nth(i, g))
                pe.wait_ge(rho_made, nth(i, g))
                for k, hs in enumerate(HEAD):
                    for b in range(2):
                        mm(by2(B.X[k][:, cols(b, 256)]), B.kappa[hs, BLK[b]], B.ar[hs, :, BLK[b]])
                        ins = mm(by2(B.X[2 + k][:, cols(b, 256)]), B.beta[hs, BLK[b]], B.ar[hs, :, BLK[b]])
                ins.then_inc(gram_made, 1)
            for g, B in BOTH:
                pe.wait_ge(gram_read, nth(i, g))
                for k, hs in enumerate(HEAD):
                    for b in range(2):
                        mm(B.X[k][:, cols(b, P)], B.ar[hs, 0, BLK[b]], B.beta[hs, BLK[b]])
                    tail = B.X[2 + k][0:TAIL]
                    mm(by2(tail[:, 0:32]), B.kappa[hs, END], B.ar[hs, :, END])
                    mm(by2(tail[:, 32:64]), B.beta[hs, END], B.ar[hs, :, END])
                    ins = mm(tail[:, 64:80], B.ar[hs, 0, END], B.beta[hs, END])
                ins.then_inc(gram2_made, 1)
            for g, B in BOTH:
                pe.wait_ge(gram2_read, nth(i, g))
                for k, hs in enumerate(HEAD):
                    for b in range(2):
                        mm(B.X[0][:, cols(2 * k + b, 64)], B.A4[:, k, b, 0:P], B.v_tok[:, b, hs])
                    ins = mm(B.X[0][0:TAIL, cols(4 + k, 64)], B.tA[:, k, 0, :], B.tV[:, hs])
                ins.then_inc(nv_summed, 1)
            for n in range(NL):
                for g, B in BOTH:
                    if n == 0:
                        pe.wait_ge(xx_made, nth(i, g))
                    pe.wait_ge(moff_made, nth(i, g, NL, n))
                    pe.wait_ge(zw_made, nth(i, g, NL + 1, n))
                    for q in range(4):
                        ins = mm(B.X[1][:, cols(q, P)], B.F4[:, q, :], B.Z4[:, q, :])
                    if n < TAIL_LEVELS:
                        for k in range(2):
                            ins = mm(B.X[0][0:TAIL, cols(k, TAIL)], B.tF[:, k, :], B.tZ[:, k, :])
                    ins.then_inc(t_summed, 1)
                for g, B in BOTH:
                    pe.wait_ge(t_copied, nth(i, g, NL, n))
                    for q in range(4):
                        ins = mm(B.X[2][:, cols(q, P)], B.W4[:, q, :], B.T4[:, q, :])
                    if n < NL - 1:
                        for q in range(4):
                            ins = mm(B.X[3][:, cols(q, P)], B.T4[:, q, :], B.W4[:, q, :])
                    if n < TAIL_LEVELS:
                        for k in range(2):
                            mm(B.X[0][0:TAIL, cols(2 + k, TAIL)], B.tW[:, k, :], B.tT[:, k, :])
                            ins = mm(B.X[0][0:TAIL, cols(4 + k, TAIL)], B.tT[:, k, :], B.tW[:, k, :])
                    ins.then_inc(zw_summed, 1)
            for g, B in BOTH:
                pe.wait_ge(zw_made, nth(i, g, NL + 1, NL))
                for k in range(2):
                    for b in range(2):
                        mm(B.X[1][:, cols(2 * k + b, P)], B.Z4[:, 2 * k + b, :], B.XX[:, k, b])
                    ins = mm(B.X[0][0:TAIL, cols(k, P)], B.tZ[:, k, :], B.tXX[:, k])
                ins.then_inc(wx_summed, 1)
            for g, B in BOTH:
                pe.wait_ge(wx_made, nth(i, g))
                for k, hs in enumerate(HEAD):
                    for b in range(2):
                        ins = mm(B.X[3][hs, BLK[b]], B.XX[:, k, b, 0, :], B.BX[:, b, k])
                ins.then_inc(g_summed, 1)
                for k, hs in enumerate(HEAD):
                    for b in range(2):
                        mm(B.X[2][hs, BLK[b]], B.XX[:, k, b, 0, :], B.B4[:, k, b, P:2 * P])
                    ins = mm(B.X[2][hs, END], B.tXX[:, k, 0, :], B.tB[:, k, 1, :])
                ins.then_inc(rq_summed, 1)
            for c in range(4):
                b, half = divmod(c, 2)
                for g, B in BOTH:
                    new = B.X[1][:, cols(c, P)]
                    if c:
                        pe.wait_ge(state_made, nth(i, g, 4, c - 1))
                    else:
                        pe.wait_ge(gbd_made, nth(i, g))
                    mm(new, B.gbd[:, c, :], B.state[:, c, :], stop=False)
                    for k, hs in enumerate(HEAD):
                        mm(new[hs, hs], B.KX[:, b, k, half, :], B.v_tok[:, b, hs], start=False, stop=False)
                        ins = mm(new[hs, hs], B.BX[:, b, k, half, :], B.XX[:, k, b, 1, :], start=False, stop=True)
                    ins.then_inc(state_summed, 1)
                    if c < 2:
                        k, hs = c, HEAD[c]
                        for b_ in range(2):
                            mm(B.X[0][hs, BLK[b_]], B.v_tok[:, b_, hs], B.A4[:, k, b_, P:2 * P], start=(b_ == 0), stop=False)
                            mm(B.X[0][hs, BLK[b_]], B.XX[:, k, b_, 1, :], B.B4[:, k, b_, P:2 * P], start=False, stop=False)
                        mm(B.X[0][hs, END], B.tV[:, hs], B.tA[:, k, 1, :], start=False, stop=False)
                        mm(B.X[0][hs, END], B.tXX[:, k, 1, :], B.tB[:, k, 1, :], start=False, stop=False)
            for g, B in BOTH:
                pe.wait_ge(state_made, nth(i, g, 4, 3))
                pe.wait_ge(rq_made, nth(i, g))
                for c in range(1, 5):
                    t = slice(CH * c, min(CH * (c + 1), T))
                    ins = mm(B.X[0][:, t], B.state[:, c, :], B.rq[:, t], start=False, stop=(c == 4))
                ins.then_inc(y_summed, 1)
            for g, B in BOTH:
                pe.wait_ge(y_copied, nth(i, g))
                mm(B.X[2][:, 0:T], head_ones, B.rk[:]).then_inc(mean_summed, 1)
            keep_warm(X[0], 2)
            for g, B in BOTH:
                pe.wait_ge(ysq_made, nth(i, g))
                mm(B.X[3][:, 0:T], head_ones, B.inv[:]).then_inc(var_summed, 1)

    def rwkv_act(act, fn):
        with act.Fori(0, PAIRS // 2) as i:
            for g, B in BOTH:
                j = i * 2 + g
                act.wait_ge(pair_out, nth(i, g))
                fn(B.kk[:], rkv[:, j + 8, :], ACT.Identity, scale=par("k_k", j))
                fn(B.inv[:], rkv[:, j + 8, :], ACT.Square, scale=par("k_k", j)).then_inc(kq_made, 1)
            for g, B in BOTH:
                j = i * 2 + g
                act.wait_ge(lora_summed, nth(i, g))
                fn(B.dk[:], B.X[0][:, 0:T], ACT.Sigmoid, bias=par("w0", j))
                fn(B.ag[:], B.X[1][:, 0:T], ACT.Sigmoid, bias=par("a0", j))
                fn(B.gg[:], B.X[2][:, 0:T], ACT.Copy).then_inc(lora_read, 1)
                act.wait_ge(lora_read, nth(i, g))
                fn(B.k2[:], B.ag[:], ACT.Identity, scale=par("k_a", j), bias=der("one_minus_ka", j)).then_inc(k2_scaled, 1)
            for g, B in BOTH:
                act.wait_ge(kk_summed, nth(i, g))
                fn(B.inv[:], B.X[3][:, 0:T], ACT.Sqrt).then_inc(kk_root, 1)
            for g, B in BOTH:
                act.wait_ge(cum_made, nth(i, g))
                fn(B.e_neg[:], B.cum[:], ACT.Exp, scale=-DECAY).then_inc(e_neg_made, 1)
                fn(B.e_pos[:], B.cum[:], ACT.Exp, scale=DECAY)
                act.wait_ge(lag_made, nth(i, g))
                fn(B.dk[:], B.dk[:], ACT.Exp, scale=-DECAY).then_inc(exps_made, 1)
            for g, B in BOTH:
                act.wait_ge(vt_turned, nth(i, g))
                fn(B.v_tok[:], by2(B.X[1][:, 0:256]), ACT.Copy)
                fn(B.tV[:], B.X[1][0:TAIL, 256:384], ACT.Copy)
            for g, B in BOTH:
                act.wait_ge(rows_turned, nth(i, g))
                for b in range(2):
                    fn(B.XX[:, :, b, 0, :], by2(B.X[2][:, cols(b, P)]), ACT.Copy)
                fn(B.tXX[:, :, 0, :], by2(B.X[2][0:TAIL, 256:384]), ACT.Copy).then_inc(rows_read_act, 1)
            for g, B in BOTH:
                act.wait_ge(nv_summed, nth(i, g))
                fn(B.XX[:].rearrange("p k b a v -> p (k b) a v")[:, :, 1, :], by4(B.X[0][:, 0:256]), ACT.Copy)
                fn(B.tXX[:, :, 1, :], by2(B.X[0][0:TAIL, 256:384]), ACT.Copy).then_inc(xx_made, 1)
            for n in range(NL):
                for g, B in BOTH:
                    act.wait_ge(t_summed, nth(i, g, NL, n))
                    ins = fn(B.T4[:], by4(B.X[1][:]), ACT.Copy)
                    if n < TAIL_LEVELS:
                        ins = fn(B.tT[:], by2(B.X[0][0:TAIL, 0:32]), ACT.Copy)
                    ins.then_inc(t_copied, 1)
            for g, B in BOTH:
                act.wait_ge(wx_summed, nth(i, g))
                fn(B.XX[:].rearrange("p k b a v -> p (k b a v)"), B.X[1][:], ACT.Copy)
                fn(B.tXX[:].rearrange("p k a v -> p (k a v)"), B.X[0][0:TAIL, 0:256], ACT.Copy).then_inc(wx_made, 1)
            for c in range(4):
                for g, B in BOTH:
                    act.wait_ge(state_summed, nth(i, g, 4, c))
                    fn(B.state[:, c + 1, :], B.X[1][:, cols(c, P)], ACT.Copy).then_inc(state_made, 1)
            for g, B in BOTH:
                act.wait_ge(y_summed, nth(i, g))
                fn(B.rk[:], B.X[0][:, 0:T], ACT.Copy).then_inc(y_copied, 1)
            for g, B in BOTH:
                act.wait_ge(centred, nth(i, g))
                fn(B.inv[:], B.kk[:], ACT.Square).then_inc(ysq_made, 1)
            for g, B in BOTH:
                act.wait_ge(var_summed, nth(i, g))
                fn(B.inv[:], B.X[3][:, 0:T], ACT.Sqrt, scale=1.0 / 64, bias=gn_eps_col).then_inc(gn_root, 1)
        act.wait_ge(pair_out, PAIRS + 2)
        split_first(make_hi, act, "out0")
        for n in range(0, PAIRS, 2):
            fn(y_hi[:, 8 + n:10 + n, :], rkv[:, n:n + 2, :], ACT.Copy).then_inc(y_hi_made, 1)

    def rwkv_pool(pool):
        def weights(g, j, B):
            c = ds(j * P, P)
            pool.dma_start(B.pair_w[0:64, 0, :], A["rwkv_w2"][0][:, c]).then_inc(pairw_landed[g], 16)
            pool.dma_start(B.pair_w[64:P, 0, :], A["rwkv_a2"][0][:, c]).then_inc(pairw_landed[g], 16)
            pool.dma_start(B.pair_w[:, 1, :], A["rwkv_g2"][0][:, c]).then_inc(pairw_landed[g], 16)

        def two_pairs(i, last):
            for g, B in BOTH:
                pool.wait_ge(pair_out, nth(i, g))
                pool.tensor_copy(B.v_loc[:], rkv[:, i * 2 + (16 + g), :]).then_inc(v_loc_made, 1)
            if not last:
                for g, B in BOTH:
                    pool.wait_ge(lora_summed, nth(i, g))
                    weights(g, i * 2 + (2 + g), B)
            for g, B in BOTH:
                pool.wait_ge(k2_scaled, nth(i, g))
                pool.tensor_tensor(B.k2[:], B.k2[:], rkv[:, i * 2 + (8 + g), :], ALU.mult).then_inc(k2_made, 1)
            for g, B in BOTH:
                pool.wait_ge(e_neg_made, nth(i, g))
                pool.tensor_tensor(B.ar[:, 1, :], rkv[:, i * 2 + g, :], B.e_neg[:], ALU.mult).then_inc(rho_made, 1)
            for n in range(NL):
                for g, B in BOTH:
                    if n:
                        pool.wait_ge(t_summed, nth(i, g, NL, n - 1))
                    else:
                        pool.wait_ge(gram2_read, nth(i, g))
                    level = rw_c[:, MASK["levels"] + n * P:MASK["levels"] + (n + 1) * P]
                    ins = pool.tensor_tensor(B.F4[:], B.M4[:], wide(level, 4), ALU.mult)
                    if n < TAIL_LEVELS:
                        ins = pool.tensor_tensor(B.tF[:], B.tM[:], wide(level[0:TAIL, 0:TAIL], 2), ALU.mult)
                    ins.then_inc(moff_made, 1)

        for g, B in BOTH:
            weights(g, g, B)
        pool.wait_ge(unit_used, UNITS * FIRST["out0"])
        pool.dma_start(rw_c[:], A["const_rwkv"]).then_inc(rwc_landed, 16)
        pool.wait_ge(rwc_landed, 16)
        with pool.Fori(0, PAIRS // 2 - 1) as i:
            two_pairs(i, False)
        two_pairs(PAIRS // 2 - 1, True)

    def rwkv_dve(dve, link, tt, stt, ts, split_y):
        for g, B in BOTH:
            link(nc.vector.memset(B.state[:, 0, :], 0.0))
        dve.sem_inc(pair_out, 2)
        dve.wait_ge(rwc_landed, 16)
        ends = slice(CH - 1, 4 * CH, CH)
        with link.loop(PAIRS // 2, RWKV_STEPS) as i:
            def r(g):
                return rkv[:, i * 2 + g, :]

            for g, B in BOTH:
                dve.wait_ge(lora_read, nth(i, g))
                nc.vector.tensor_tensor_scan(B.cum[:], mask("restart", T), B.dk[:], 0.0, ALU.mult, ALU.add).then_inc(
                    cum_made, 1)
                dve.wait_ge(cum_made, nth(i, g))
                tt(B.dk[:], B.cum[:], B.dk[:], ALU.subtract).then_inc(lag_made, 1)
            for g, B in BOTH:
                dve.wait_ge(kk_root, nth(i, g))
                link(ts(B.inv[:], B.inv[:], 1e-12, None, ALU.max))
                link(nc.vector.reciprocal(B.inv[:], B.inv[:]))
            for g, B in BOTH:
                link(tt(B.kk[:], B.kk[:], B.inv[:], ALU.mult))
                dve.wait_ge(k2_made, nth(i, g))
                stt(B.rk[:], r(g), par("r_k", i * 2 + g), B.k2[:], ALU.mult, ALU.mult).then_inc(rk_made, 1)
            for g, B in BOTH:
                dve.wait_ge(exps_made, nth(i, g))
                tt(B.ar[:, 0, :], B.kk[:], B.dk[:], ALU.mult)
                link(tt(B.inv[:], B.kk[:], B.ag[:], ALU.mult))
                tt(B.beta[:], B.inv[:], B.e_pos[:], ALU.mult)
                link(tt(B.kappa[:], B.k2[:], B.e_pos[:], ALU.mult))
                whole = B.e_neg[:, ends].unsqueeze(2).broadcast_to([P, 4, CH])

                def chunked(ap):
                    return ap.rearrange("p (c t) -> p c t", t=CH)
                tt(chunked(B.beta_end[:]), chunked(B.beta[:, 0:256]), whole, ALU.mult)
                tt(chunked(B.kappa_end[:]), chunked(B.kappa[:, 0:256]), whole, ALU.mult).then_inc(feats_made, 1)
            for g, B in BOTH:
                dve.wait_ge(bonus_summed, nth(i, g))
                tt(B.cum[:], B.X[0][:, 0:T], rkv[:, i * 2 + (16 + g), :], ALU.mult).then_inc(bonus_read, 1)
                dve.wait_ge(rows_turned, nth(i, g))

                def by_chunk(ap):
                    return ap.rearrange("p (q v) -> p q v", q=4).unsqueeze(2).broadcast_to([P, 4, 2, 64])

                def chunk_mask(name):
                    return mask(name, 2).unsqueeze(1).unsqueeze(3).broadcast_to([P, 4, 2, 64])
                tt(B.BX[:].rearrange("p b k c v -> p (b k) c v"), by_chunk(B.X[3][:, 0:256]), chunk_mask("nchunk"), ALU.mult)
                tt(B.KX[:].rearrange("p b k c v -> p (b k) c v"), by_chunk(B.X[3][:, 256:512]), chunk_mask("chunk"),
                   ALU.mult).then_inc(rows_read_dve, 1)
            for g, B in BOTH:
                dve.wait_ge(gram_made, nth(i, g))
                for k in range(2):
                    tt(B.A4[:, k], by2(B.X[k][:]), wide(mask("A", 256)), ALU.mult)
                    ins = tt(B.B4[:, k], by2(B.X[2 + k][:]), wide(mask("B", 256)), ALU.mult)
                ins.then_inc(gram_read, 1)
            for g, B in BOTH:
                dve.wait_ge(gram2_made, nth(i, g))
                for k in range(2):
                    tt(B.M4[:, 2 * k:2 * k + 2, :], by2(B.X[k][:, 0:256]), wide(mask("M")), ALU.mult)
                    tail = B.X[2 + k][0:TAIL]
                    for dst, c, name in ((B.tA, 0, "A"), (B.tB, 32, "B")):
                        m = by2(mask(name, 256, TAIL))[:, :, 0:TAIL]
                        tt(dst[:, k], by2(tail[:, c:c + 32]), m, ALU.mult)
                    ins = tt(B.tM[:, k, :], tail[:, 64:80], mask("M", TAIL, TAIL), ALU.mult)
                ins.then_inc(gram2_read, 1)
            for g, B in BOTH:
                dve.wait_ge(gram2_read, nth(i, g))
                E4 = B.B4[:].rearrange("p k b t -> p (k b) t")[:, :, 0:P]
                tt(B.W4[:], B.M4[:], wide(mask("pair"), 4), ALU.mult)
                tt(B.Z4[:], E4, wide(mask("pairT"), 4), ALU.mult)
                tt(B.tW[:], B.tM[:], wide(mask("pair", TAIL, TAIL)), ALU.mult)
                link(tt(B.tZ[:], B.tB[:, :, 0, :], wide(mask("pairT", TAIL, TAIL)), ALU.mult))
                tt(B.W4[:], wide(ident, 4), B.W4[:], ALU.subtract)
                tt(B.Z4[:], wide(ident, 4), B.Z4[:], ALU.subtract)
                tt(B.tW[:], wide(ident[0:TAIL, 0:TAIL]), B.tW[:], ALU.subtract)
                tt(B.tZ[:], wide(ident[0:TAIL, 0:TAIL]), B.tZ[:], ALU.subtract).then_inc(zw_made, 1)
            for n in range(NL):
                for g, B in BOTH:
                    dve.wait_ge(zw_summed, nth(i, g, NL, n))
                    dve.wait_ge(zw_made, nth(i, g, NL + 1, n))
                    ins = tt(B.Z4[:], B.Z4[:], by4(B.X[2][:]), ALU.subtract)
                    if n < TAIL_LEVELS:
                        tt(B.tZ[:], B.tZ[:], by2(B.X[0][0:TAIL, 32:64]), ALU.subtract)
                        tt(B.tW[:], B.tW[:], by2(B.X[0][0:TAIL, 64:96]), ALU.subtract)
                    if n < NL - 1:
                        ins = tt(B.W4[:], B.W4[:], by4(B.X[3][:]), ALU.subtract)
                    ins.then_inc(zw_made, 1)
            for g, B in BOTH:
                nc.vector.memset(B.gbd[:], 0.0)
                for hs in HEAD:
                    ins = tt(B.dci[hs], wide(ident[hs, hs], 4), B.e_neg[hs, ends].unsqueeze(2).broadcast_to([64, 4, 64]),
                             ALU.mult)
                link(ins)
            for g, B in BOTH:
                dve.wait_ge(g_summed, nth(i, g))
                for hs in HEAD:
                    ins = tt(B.gbd[hs, :, hs], by4(B.X[3][hs, 0:256]), B.dci[hs], ALU.add)
                ins.then_inc(gbd_made, 1)
            for g, B in BOTH:
                dve.wait_ge(rq_summed, nth(i, g))
                tt(B.rq[:], B.ar[:, 1, :], B.X[2][:, 0:T], ALU.add).then_inc(rq_made, 1)
            for g, B in BOTH:
                dve.wait_ge(mean_summed, nth(i, g))
                stt(B.kk[:], B.X[2][:, 0:T], -1.0 / 64, B.rk[:], ALU.mult, ALU.add).then_inc(centred, 1)
            for g, B in BOTH:
                dve.wait_ge(gn_root, nth(i, g))
                link(nc.vector.reciprocal(B.inv[:], B.inv[:]))
                link(tt(B.kk[:], B.kk[:], B.inv[:], ALU.mult))
                link(ts(B.kk[:], B.kk[:], par("ln_w", i * 2 + g), par("ln_b", i * 2 + g), ALU.mult, ALU.add))
                link(tt(B.kk[:], B.kk[:], B.cum[:], ALU.add))
                tt(r(g), B.kk[:], B.gg[:], ALU.mult).then_inc(pair_out, 1)
        split_first(make_lo, dve, "out0")
        for n in range(0, PAIRS, 2):
            split_y(slice(8 + n, 10 + n), rkv[:, n:n + 2, :], LRU_WIDTH // PANEL + 1 + n // 2)

    RWKV_STEPS = 22

    (glc_landed, gdw_landed, gdw_made, gd_summed, gd_made, gkw_landed, gk_summed, logits_made, soft_made, gk_made, k_copied,
     v_turned, v_rows_made, diff_made, lev_exp, lev_made, score_summed, score_read, parts_added, o_summed, o_squared,
     on_summed, on_root, o_scaled, silu_made, o_made) = sems(
        "glc_landed gdw_landed gdw_made gd_summed gd_made gkw_landed gk_summed logits_made soft_made gk_made k_copied "
        "v_turned v_rows_made diff_made lev_exp lev_made score_summed score_read parts_added o_summed o_squared "
        "on_summed on_root o_scaled silu_made o_made")
    HEADS = GLA_KW // GLA_DK
    SIZES = GLA_LEVELS + (P, 2 * P)
    NS = len(SIZES) + 1
    LEVELS_OF = {6: [1, 2]} | {s + 4: [s] for s in range(3, NS - 2)} | {NS + 2: [NS - 2, NS - 1]}

    def halves(ap, size):
        if size == 2 * P:
            left, right, ref = ap[:, :, 0:size], ap[:, :, size:T], ap[:, :, size - 1:size]
            return (left, ref.broadcast_to([P, 2, size])), (right, ref.broadcast_to([P, 2, TAIL]))
        n = (T if 2 * size <= TAIL else 2 * P) // (2 * size)
        v = ap[:, :, 0:n * 2 * size].rearrange("p d (n a t) -> p d n a t", a=2, t=size)
        ref = v[:, :, :, 0, size - 1:size].broadcast_to([P, 2, n, size])
        return (v[:, :, :, 0, :], ref), (v[:, :, :, 1, :], ref)

    def gla_pe(pe, mm, turn):
        pe.wait_ge(gdw_made, 1)
        for k in range(KT):
            ins = mm(X[0][0:16, 0:T], gd_w[:, k, :], h[:, k, :], start=(k == 0), stop=(k == KT - 1))
        ins.then_inc(gd_summed, 1)
        pe.wait_ge(gd_made, 1)

        def scores(hd, s):
            out = X[2 + s % 2]
            if s:
                pe.wait_ge(lev_made, hd * (NS - 1) + s)
                left, right = levs[s % 2], levs[s % 2]
            else:
                pe.wait_ge(k_copied, hd + 1)
                left, right = k_loc, None
            if s > 1:
                pe.wait_ge(score_read, hd * NS + (s - 1))
            size = SIZES[s - 1] if s else 0
            if size == 2 * P:
                places = [(out[:, 0:TAIL], BLK[0], END), (out[:, TAIL:2 * TAIL], BLK[1], END)]
            elif size == P:
                places = [(out[:, 0:P], BLK[0], BLK[1])]
            else:
                places = [(out[:, 0:P], BLK[0], BLK[0]), (out[:, P:2 * P], BLK[1], BLK[1])]
                if 2 * size <= TAIL:
                    places.append((out[0:TAIL, 2 * P:2 * P + TAIL], END, END))
            for dst, sb_, tb in places:
                for d in range(2):
                    rhs = right[:, d, tb] if s else qk[:, hd * 2 + d, tb]
                    ins = mm(dst, left[:, d, sb_], rhs, start=(d == 0), stop=(d == 1))
            ins.then_inc(score_summed, 1)

        def step(slot, hd):
            if slot == 0:
                pe.wait_ge(o_scaled, hd + 1)
                pe.wait_ge(gkw_landed, hd * 16 + 16)
                for n in range(2):
                    ins = mm(X[n][:, 0:T], gk_w[:, cols(n, P)], gd_t[:])
                ins.then_inc(gk_summed, 1)
            if slot == 1:
                scores(hd, 0)
            for s in LEVELS_OF.get(slot, ()):
                scores(hd, s)
            if slot == 8:
                wait_drained(pe, "gla_vg", 1, hd)
                pe.wait_ge(logits_made, hd + 1)
                for b in range(2):
                    for m in range(4):
                        ins = turn(X[b][:, cols(m, P)], v_in[:, m, BLK[b]])
                ins.then_inc(v_turned, 1)
            if slot == 9:
                pe.wait_ge(v_rows_made, hd * 2 + 1)
                for m in range(4):
                    ins = turn(X[0][0:TAIL, cols(m, P)], v_in[:, m, END])
                ins.then_inc(v_turned, 1)
            if slot == 13:
                pe.wait_ge(v_rows_made, hd * 2 + 2)
                pe.wait_ge(score_read, hd * NS + NS)
                pe.wait_ge(parts_added, hd * len(GLA_LEVELS) + len(GLA_LEVELS))
                for m in range(4):
                    mm(X[m][:, 0:T], v_rows[:, 0, cols(m, P)], at0[:], stop=False)
                    mm(X[m][:, P:T], v_rows[:, 1, cols(m, P)], at1[:], start=False, stop=False)
                    ins = mm(X[m][:, END], v_rows[0:TAIL, 2, cols(m, P)], at2[:], start=False)
                ins.then_inc(o_summed, 1)
            if slot == 14:
                pe.wait_ge(o_squared, hd + 1)
                for m in range(4):
                    ins = mm(X[0][:, 0:T], ones, gsq[:, m, :], start=(m == 0), stop=(m == 3))
                ins.then_inc(on_summed, 1)
        return step

    def gla_act(act, fn):
        def step(slot, hd):
            if slot == 1:
                act.wait_ge(logits_made, hd + 1)
                fn(soft[:], logits[:], ACT.Abs).then_inc(soft_made, 1)
                act.wait_ge(soft_made, hd * 3 + 1)
                fn(soft[:], soft[:], ACT.Exp, scale=-1.0).then_inc(soft_made, 1)
                act.wait_ge(soft_made, hd * 3 + 2)
                fn(soft[:], soft[:], ACT.Ln, bias=1.0).then_inc(soft_made, 1)
            for s in LEVELS_OF.get(slot, ()):
                act.wait_ge(diff_made, hd * (NS - 1) + s)
                if s > 2:
                    act.wait_ge(score_summed, hd * NS + (s - 1))
                n = T if 2 * SIZES[s - 1] <= TAIL or SIZES[s - 1] == 2 * P else 2 * P
                fn(levs[s % 2][:, :, 0:n], diffs[s % 2][:, :, 0:n], ACT.Exp, scale=1.0 / 16).then_inc(lev_exp, 1)
            if slot == 9:
                act.wait_ge(v_turned, hd * 2 + 1)
                fn(v_rows[:, 0, :], X[0][:], ACT.Copy)
                fn(v_rows[:, 1, :], X[1][:], ACT.Copy).then_inc(v_rows_made, 1)
            if slot == 10:
                act.wait_ge(v_turned, hd * 2 + 2)
                fn(v_rows[0:TAIL, 2, :], X[0][0:TAIL, :], ACT.Copy).then_inc(v_rows_made, 1)
            if slot == 14:
                act.wait_ge(o_summed, hd + 1)
                fn(o_all[:, 0, :], X[0][:, 0:T], ACT.Copy)
                for m in range(4):
                    ins = fn(gsq[:, m, :], X[m][:, 0:T], ACT.Square)
                ins.then_inc(o_squared, 1)
            if slot == 15:
                act.wait_ge(on_summed, hd + 1)
                fn(gr[:], X[0][:, 0:T], ACT.Sqrt, scale=1.0 / GLA_DV, bias=eps_col).then_inc(on_root, 1)

        def drain(p, hd):
            if p == 3:
                wait_drained(act, "gla_vg", 3, hd)
                fn(g_loc[:], g_loc[:], ACT.Silu).then_inc(silu_made, 1)
        return step, drain

    def gla_pool(pool):
        pool.wait_ge(pre_root, 3)
        pool.dma_start(gd_w[:], A["gla_w_in"][0].rearrange("(k p) n -> p k n", p=P)[:, :, 2 * GLA_KW + 2 * GLA_VW:]).then_inc(
            gdw_landed, 16)
        pool.wait_ge(unit_used, UNITS * FIRST["gla_qk"])
        pool.dma_start(gl_c[:], A["const_gla"].rearrange("p (a b) -> p a b", a=8)).then_inc(glc_landed, 16)

        def weights(hd):
            pool.dma_start(gk_w[:], A["gla_gk_up"][0][:, ds(hd * GLA_DK, GLA_DK)]).then_inc(gkw_landed, 16)

        def head(hd, last):
            pool.wait_ge(o_scaled, hd + 1)
            pool.tensor_copy(k_loc[:], qk[:, ds(hd * 2 + 8, 2), :]).then_inc(k_copied, 1)
            pool.wait_ge(gk_made, hd * 2 + 2)
            if not last:
                weights(hd + 1)

            def add(s):
                pool.wait_ge(score_read, hd * NS + (s + 1))
                pool.tensor_tensor(at0[:, 0:P], at0[:, 0:P], part[:, 0, :], ALU.add)
                ins = pool.tensor_tensor(at1[:, 0:P], at1[:, 0:P], part[:, 1, :], ALU.add)
                if 2 * SIZES[s - 1] <= TAIL:
                    ins = pool.tensor_tensor(at2[:], at2[:], part2[:], ALU.add)
                ins.then_inc(parts_added, 1)

            for s in range(1, NS):
                if s > 2:
                    pool.wait_ge(lev_exp, hd * (NS - 1) + (s - 2))
                (left, ref), (right, ref_r) = halves(gk[:], SIZES[s - 1])
                (dl, _), (dr, _) = halves(diffs[s % 2][:], SIZES[s - 1])
                for d in range(2):
                    pool.tensor_tensor(dl[:, d], ref[:, d], left[:, d], ALU.subtract)
                    ins = pool.tensor_tensor(dr[:, d], right[:, d], ref_r[:, d], ALU.subtract)
                ins.then_inc(diff_made, 1)
                if 3 <= s <= len(GLA_LEVELS) + 2:
                    if s > 3:
                        pool.wait_ge(parts_added, hd * len(GLA_LEVELS) + (s - 3))
                    add(s - 2)

        weights(0)
        with pool.Fori(0, HEADS - 1) as hd:
            head(hd, False)
        head(HEADS - 1, True)

    def gla_dve(dve, link, tt, stt, ts, scaled):
        dve.wait_ge(gd_summed, 1)
        tt(gd_t[:], X[0][0:16, 0:T], rpre[0:16, :], ALU.mult).then_inc(gd_made, 1)
        dve.wait_ge(glc_landed, 16)
        dve.sem_inc(o_scaled, 1)
        NG = len(GLA_LEVELS)
        scale = GLA_DK ** -0.5

        def read_scores(hd, s):
            dve.wait_ge(score_summed, hd * NS + (s + 1))
            src = X[2 + s % 2]
            size = SIZES[s - 1] if s else 0
            if size == 2 * P:
                ts(at0[:, END], src[:, 0:TAIL], scale, None, ALU.mult)
                ts(at1[:, P:P + TAIL], src[:, TAIL:2 * TAIL], scale, None, ALU.mult).then_inc(score_read, 1)
                return
            if size == P:
                ts(at0[:, BLK[1]], src[:, 0:P], scale, None, ALU.mult).then_inc(score_read, 1)
                return
            m = gl_c[:, s, :]
            if s == 0:
                tt(at0[:, 0:P], src[:, 0:P], m, ALU.mult)
                tt(at1[:, 0:P], src[:, P:2 * P], m, ALU.mult)
                tt(at2[:], src[0:TAIL, 2 * P:2 * P + TAIL], m[0:TAIL, 0:TAIL], ALU.mult).then_inc(score_read, 1)
                return
            if s > 1:
                dve.wait_ge(parts_added, hd * NG + (s - 1))
            if 2 * size <= TAIL:
                tt(part2[:], src[0:TAIL, 2 * P:2 * P + TAIL], m[0:TAIL, 0:TAIL], ALU.mult)
            tt(part[:], src[:, 0:2 * P].rearrange("p (a t) -> p a t", a=2), wide(m), ALU.mult).then_inc(score_read, 1)

        def step(slot, hd):
            if slot == 1:
                dve.wait_ge(gk_summed, hd + 1)
                for n in range(2):
                    ins = ts(logits[:, n, :], X[n][:, 0:T], par("gk_b", hd * 2 + n), None, ALU.add)
                ins.then_inc(logits_made, 1)
            if slot == 2:
                dve.wait_ge(soft_made, hd * 3 + 3)
                link(stt(soft[:], logits[:], 0.0, soft[:], ALU.min, ALU.subtract))
                for n in range(2):
                    nc.vector.tensor_tensor_scan(gk[:, n, :], ones[:, 0:1].broadcast_to([P, T]), soft[:, n, :], 0.0,
                                                 ALU.mult, ALU.add).then_inc(gk_made, 1)
                read_scores(hd, 0)
                dve.wait_ge(k_copied, hd + 1)
            for s in LEVELS_OF.get(slot, ()):
                dve.wait_ge(lev_exp, hd * (NS - 1) + s)
                (ll, _), (lr, _) = halves(levs[s % 2][:], SIZES[s - 1])
                (kl, _), _ = halves(k_loc[:], SIZES[s - 1])
                _, (qr, _) = halves(qk[:, ds(hd * 2, 2), :], SIZES[s - 1])
                tt(ll, ll, kl, ALU.mult)
                tt(lr, lr, qr, ALU.mult).then_inc(lev_made, 1)
                if s > 1:
                    read_scores(hd, s - 1)
            if slot == 13:
                read_scores(hd, NS - 1)
            if slot == 15:
                dve.wait_ge(on_root, hd + 1)
                link(nc.vector.reciprocal(gr[:], gr[:]))
                for m in range(4):
                    src = X[m][:, 0:T] if m else o_all[:, 0, :]
                    ins = stt(o_all[:, m, :], src, par("gla_nw", m), gr[:], ALU.mult, ALU.mult)
                ins.then_inc(o_scaled, 1)

        def drain(p, hd):
            scaled((v_in, g_loc)[p // 2][:, 2 * (p % 2):2 * (p % 2) + 2, :], "gla_vg", p, hd)
            if p == 3:
                dve.wait_ge(silu_made, hd + 1)
                dve.wait_ge(o_scaled, hd + 2)
                tt(o_gated[:, ds(hd * 4, 4), :], o_all[:], g_loc[:], ALU.mult).then_inc(o_made, 1)
        return step, drain

    GLA_STEPS = 2

    def load_params(engine, share):
        for src, group, row, count in list(param_pieces(A))[share::3]:
            engine.dma_start(par_rows[row:row + count, group, :], src).then_inc(params_landed[share], 16)

    block = ctx.enter_context(nc.Block())

    @block.sync
    def _(sp):
        sp.dma_start(trunk_c[:], A["const_trunk"].rearrange("p (a b) -> p a b", a=3)).then_inc(trunk_landed, 16)
        sp.dma_start(x_tok[:], A["x"][0].rearrange("(b p) d -> p b d", p=P)).then_inc(inputs_landed, 16)
        sp.dma_start(meta_tok[:], A["meta_tokens"]).then_inc(inputs_landed, 16)
        load_params(sp, 0)

        for name, iters, panels in plan:
            first, per = FIRST[name] * UNITS, len(panels) * UNITS

            def iteration(i):
                for p, (w, c0, step, k0, kn) in enumerate(panels):
                    for u in range(UNITS):
                        unit = first + p * UNITS + u
                        slot = unit % RAW_SLOTS
                        if not isinstance(i, int):
                            sp.wait_ge(lo_made, i * per + (unit - RAW_SLOTS + 1))
                        elif unit + per * i >= RAW_SLOTS:
                            sp.wait_ge(lo_made, unit + per * i - RAW_SLOTS + 1)
                        k = k0 // P + u * kn
                        sp.dma_start(raw[:, slot, 0:kn, :],
                                     views[w][:, k:k + kn, ds(i * step + c0, PANEL)]).then_inc(raw_landed[slot], 16)

            start = 0
            while start < iters and first + start * per < RAW_SLOTS:
                iteration(start)
                start += 1
            if iters > start:
                with sp.Fori(start, iters) as i:
                    iteration(i)

        for g in range(4):
            sp.wait_ge(out_copied, 2 * (g + 1))
            c = slice(g * 512, (g + 1) * 512)
            sp.dma_start(A["out"][0].rearrange("(b p) d -> p b d", p=P)[:, :, c], out_tok[:, :, c]).then_inc(out_landed, 16)
        sp.wait_ge(out_landed, 64)

    def make_hi(act, unit, i, per):
        if isinstance(i, int):
            unit, i = unit + per * i, 0
            if unit >= TOTAL_UNITS:
                return
        slot = unit % RAW_SLOTS
        act.wait_ge(raw_landed[slot], i * (16 * per // RAW_SLOTS) + 16 * (unit // RAW_SLOTS + 1))
        if unit >= SPLIT_SLOTS:
            act.wait_ge(unit_used, i * per + (unit - SPLIT_SLOTS + 1))
        nc.scalar.activation(w_hi[:, unit % SPLIT_SLOTS], raw[:, slot], ACT.Copy).then_inc(hi_made, 1)

    def make_lo(dve, unit, i, per):
        if isinstance(i, int):
            unit, i = unit + per * i, 0
            if unit >= TOTAL_UNITS:
                return
        dve.wait_ge(hi_made, i * per + (unit + 1))
        nc.vector.tensor_tensor(w_lo[:, unit % SPLIT_SLOTS], raw[:, unit % RAW_SLOTS],
                                w_hi[:, unit % SPLIT_SLOTS].bitcast(F32), ALU.subtract).then_inc(lo_made, 1)

    def split_ahead(make, engine, name, p, i, step=None):
        iters, panels = PLAN[name]
        whole = isinstance(i, int)
        last = name in PEELED and whole and i == iters - 1 and p == len(panels) - 1
        early = name in FRESH and whole and i == 0 and p == 0
        for u in range(UNITS):
            if (u > 0 or not early) and (u == 0 or not last):
                make(engine, UNITS * (FIRST[name] + p) + u + 3, i, len(panels) * UNITS)
            if step:
                step(UNITS * p + u, i)

    def split_before_norm(make, engine, t):
        name = next(n for n, k in FRESH.items() if k == t)
        make(engine, UNITS * FIRST[name] + 3, 0, 0)

    def split_first(make, engine, name):
        for u in range(3):
            make(engine, UNITS * FIRST[name] + u, 0, 0)

    @block.tensor
    def _(pe):
        def mm(out, lhsT, rhs, start=True, stop=True, **k):
            return nc.tensor.matmul(out, lhsT, rhs, start=start, stop=stop, **k)

        def turn(out, in_, rows=P):
            return nc.tensor.transpose(out, in_, trunk_c[0:rows, 0, 0:rows])

        def stream(name, hi, lo, ready, step=None):
            _, panels = PLAN[name]
            per = len(panels)

            def body(i):
                whole = isinstance(i, int)
                for p in range(per):
                    kn = panels[p][4]
                    n, j = FIRST[name] + p, i
                    if whole:
                        n, j = n + per * i, 0
                    first = whole and i == 0 and p == 0
                    t0 = first_token(name, p)
                    ps = main_ps[n % 2]
                    if n >= 2:
                        pe.wait_ge(drained[n % 2], j * (max(per, 2) // 2) + n // 2)
                    for u in range(UNITS):
                        unit = UNITS * n + u
                        pe.wait_ge(lo_made, j * (per * UNITS) + (unit + 1))
                        if first:
                            order = [(m, k) for k in range(kn) for m in range(2)]
                        else:
                            order = [(m, k) for m in range(2) for k in range(kn)]
                        for m, k in order:
                            if first and m == 0:
                                ready(u * kn + k)
                            for a, b in ((w_hi, hi), (w_lo, hi), (w_hi, lo)):
                                ins = mm(ps[:, m, t0:T], a[:, unit % SPLIT_SLOTS, k, m * P:(m + 1) * P],
                                         b[:, u * kn + k, t0:T],
                                         start=(u == 0 and k == 0 and a is w_hi and b is hi),
                                         stop=(u == UNITS - 1 and k == kn - 1 and b is lo))
                        ins.then_inc(unit_used, 1)
                        if step:
                            step(UNITS * p + u, i)
                    if first and name in FRESH:
                        pe.wait_ge(h_added, (KT - 1) * (FRESH[name] + 1))
                        t0 = FROM_IN[FRESH[name]]
                        mm(X[1][:, t0:T], ones, h_sum[:, t0:T]).then_inc(pre_sum, 1)

            iterations(pe.Fori, name, body, True)

        def x_stream(name, t, **k):
            def ready(m):
                if name in FRESH:
                    pe.wait_ge(x_lo_made, KT * t + m + 1)
            stream(name, x_hi, x_lo, ready, **k)

        def y_stream(name):
            def ready(m):
                if m % 2 == 0:
                    pe.wait_ge(y_lo_made, Y_BEFORE[name] + m // 2 + 1)
            stream(name, y_hi, y_lo, ready)

        def post_norm(t):
            pe.wait_ge(added, 20 * t)
            t0 = FROM_OUT[t - 1]
            mm(X[0][:, t0:T], ones, acc[:, t0:T]).then_inc(post_sum, 1)

        pe.wait_ge(trunk_landed, 16)
        pe.wait_ge(inputs_landed, 32)
        for k in range(KT):
            dst = X[2 + k % 2]
            if k >= 2:
                pe.wait_ge(h_ready, k - 1)
            cols = slice(k * P, (k + 1) * P)
            turn(dst[:, 0:N_META], meta_tok[:, cols], N_META)
            turn(dst[:, N_META:N_META + P], x_tok[:, 0, cols])
            turn(dst[:, N_META + P:T], x_tok[:, 1, cols]).then_inc(h_turned, 1)
        for share in range(3):
            pe.wait_ge(params_landed[share], 16 * len(range(share, N_PARAM_DMAS, 3)))
        for g in range(PT_GROUPS):
            ins = turn(X[g // 4][:, (g % 4) * P:(g % 4 + 1) * P], par_rows[:, g, :])
        ins.then_inc(par_turned, 1)
        pe.wait_ge(params_ready, 1)

        x_stream("wag", 0)
        x_stream("rkv", 0)

        def lru_gates(slot, i):
            if slot != 5:
                return
            pe.wait_ge(gatew_landed, i * 64 + 64)
            pe.wait_ge(lx_made, i + 1)
            for n in range(4):
                ins = mm(X[n][:, 0:T], gate_w[:, n, :], lx[:, n % 2, :])
            ins.then_inc(gates_summed, 1)

        x_stream("lru", 0, step=lru_gates)
        rwkv_pe(pe, mm, turn)
        y_stream("out0")
        post_norm(1)

        def ffn(layer):
            for n in range(3):
                x_stream(f"gv{layer}_{n}", 2 * layer + 1)
                y_stream(f"dn{layer}_{n}")
            post_norm(2 * layer + 2)

        if upto >= 2:
            ffn(0)
        if upto >= 3:
            x_stream("gla_qk", 2)
            x_stream("gla_vg", 2, step=gla_pe(pe, mm, turn))
            y_stream("out1")
            post_norm(3)
        if upto >= 4:
            ffn(1)
        for n in range(8):
            g, b = divmod(n, 2)
            pe.wait_ge(h_ready, KT * upto + 4 * (g + 1))
            if n >= 4:
                pe.wait_ge(out_copied, n - 3)
            for k in range(4):
                c = N_META + b * P
                ins = turn(X[n % 4][:, k * P:(k + 1) * P], h[:, 4 * g + k, c:c + P])
            ins.then_inc(out_turned, 1)

    @block.scalar
    def _(act):
        link = Chain(act, act_chain)

        def fn(out, in_, f, **k):
            return nc.scalar.activation(out, in_, f, **k)

        def load_table(f):
            n = N_DCOLS + 2 + (ACT.Sqrt, ACT.Sigmoid, ACT.Gelu_apprx_tanh).index(f)
            fn(derived[:, n:n + 1], ones[:, 0:1], f)

        def stream(name, drain, step=None):
            def body(i):
                for p in range(len(PLAN[name][1])):
                    split_ahead(make_hi, act, name, p, i, step)
                    if name in FRESH and isinstance(i, int) and i == 0 and p == 0:
                        act.wait_ge(pre_sum, FRESH[name] + 1)
                        t0 = FROM_IN[FRESH[name]]
                        fn(root[:, t0:T], X[1][:, t0:T], ACT.Sqrt, scale=1.0 / D_MODEL, bias=eps_col).then_inc(pre_root, 1)
                    drain(p, i)
            iterations(act.Fori, name, body, name in FRESH)

        def nothing(p, i):
            pass

        def transition(t):
            if t < upto:
                split_before_norm(make_hi, act, t)
            if t > 0:
                act.wait_ge(post_sum, t)
                t0 = FROM_OUT[t - 1]
                fn(root[:, t0:T], X[0][:, t0:T], ACT.Sqrt, scale=1.0 / D_MODEL, bias=eps_col).then_inc(post_root, 1)
            if t < upto:
                t0 = FROM_IN[t]
                with act.Fori(0, KT) as m:
                    act.wait_ge(h_ready, m + (KT * t + 1))
                    fn(x_hi[:, m, t0:T], h[:, m, t0:T], ACT.Identity, scale=pre_w(t, m)).then_inc(x_hi_made, 1)
                    fn(mo[:, m, t0:T], h[:, m, t0:T], ACT.Square).then_inc(h_squared, 1)

        load_params(act, 1)
        for k in range(KT):
            act.wait_ge(h_turned, k + 1)
            fn(h[:, k, :], X[2 + k % 2][:, 0:T], ACT.Copy).then_inc(h_ready, 1)
        split_first(make_hi, act, "wag")
        act.wait_ge(params_ready, 1)
        transition(0)

        stream("wag", nothing)
        link(fn(derived[:, 34:42], par("lam", 0, 8), ACT.Abs))
        fn(derived[:, 42:50], derived[:, 34:42], ACT.Exp, scale=-1.0).then_inc(lam_exp, 1)
        act.wait_ge(lora_in, 1)
        link(fn(lora[0:64, 0, :], lora[0:64, 0, :], ACT.Tanh))
        fn(lora[:, 1, :], lora[:, 1, :], ACT.Sigmoid).then_inc(lora_made, 1)
        stream("rkv", nothing)

        def lru_step(slot, i):
            if slot == 6:
                load_table(ACT.Sigmoid)
                act.wait_ge(gates_summed, i + 1)
                for m in range(2):
                    fn(rg[:, m, :], X[m][:, 0:T], ACT.Sigmoid, bias=par("ga_b", i * 2 + m))
                    last = fn(ig[:, m, :], X[2 + m][:, 0:T], ACT.Sigmoid, bias=par("gx_b", i * 2 + m))
                last.then_inc(gates_made, 1)
                act.wait_ge(gates_made, i + 1)
                for m in range(2):
                    fn(aa[:, m, :], rg[:, m, :], ACT.Exp, scale=der("neg8sp", i * 2 + m))
                for m in range(2):
                    last = fn(th[:, m, :], rg[:, m, :], ACT.Tanh, scale=der("pos8sp", i * 2 + m))
                last.then_inc(decays_made, 1)
            if slot == 7:
                load_table(ACT.Sqrt)
                act.wait_ge(lru_root_in, i + 1)
                fn(th[:], th[:], ACT.Sqrt).then_inc(lru_root, 1)
                load_table(ACT.Gelu_apprx_tanh)

        def lru(p, i):
            if p == 0:
                return
            wait_drained(act, "lru", 1, i)
            fn(ly[:], ly[:], ACT.Gelu_apprx_tanh).then_inc(lru_gelu, 1)
            act.wait_ge(lru_made, i + 1)
            fn(y_hi[:, ds(i * 2, 2), :], lx[:], ACT.Copy).then_inc(y_hi_made, 1)

        stream("lru", lru, lru_step)
        rwkv_act(act, fn)

        def project(t, from_mo):
            def drain(p, i):
                name = SUBLAYERS[t][3]
                tile = i * 4 + 2 * p
                t0 = FROM_OUT[t]
                act.wait_ge(added, i * 4 + (20 * t + 2 * p + 2))
                if from_mo:
                    wait_drained(act, name, p, i)
                    fn(sq[:, p, :, t0:T], mo[:, ds(tile, 2), t0:T], ACT.Square).then_inc(squared, 1)
                else:
                    wait_panel(act, name, p, i)
                    fn(sq[:, p, :, t0:T], bank(FIRST[name] + p, t0), ACT.Square).then_inc(squared, 1)
                    fn(mo[:, ds(tile, 2), t0:T], bank(FIRST[name] + p, t0), ACT.Copy).then_inc(drained[(FIRST[name] + p) % 2], 1)
            return drain

        stream("out0", project(0, False))
        transition(1)

        def ffn(layer):
            for n in range(3):
                name = f"gv{layer}_{n}"

                def gate_value(p, i, name=name):
                    c, t0 = GV_COUNT[name], first_token(name, 1)
                    if p == 0:
                        act.wait_ge(conv_made, i + (c + 1))
                        fn(gelu[:, :, t0:T], conv[:, :, t0:T], ACT.Gelu_apprx_tanh).then_inc(gelu_made, 1)
                    else:
                        act.wait_ge(prod_made, i + (c + 1))
                        fn(y_hi[:, ds(i * 2, 2), t0:T], prod[:, :, t0:T], ACT.Copy).then_inc(y_hi_made, 1)

                stream(name, gate_value)

                def first_sum(p, i, name=f"dn{layer}_0"):
                    wait_panel(act, name, p, i)
                    t0 = first_token(name)
                    fn(mo[:, ds(i * 4 + 2 * p, 2), t0:T], bank(FIRST[name] + p, t0), ACT.Copy).then_inc(
                        drained[(FIRST[name] + p) % 2], 1)

                stream(f"dn{layer}_{n}", (first_sum, nothing, project(2 * layer + 1, True))[n])
            transition(2 * layer + 2)

        if upto >= 2:
            ffn(0)
        if upto >= 3:
            stream("gla_qk", nothing)
            head_step, head_end = gla_act(act, fn)
            stream("gla_vg", head_end, head_step)
            act.wait_ge(o_made, HEADS)
            for m in range(0, KT, 2):
                fn(y_hi[:, m:m + 2, :], o_gated[:, m:m + 2, :], ACT.Copy).then_inc(y_hi_made, 1)
            stream("out1", project(2, False))
            transition(3)
        if upto >= 4:
            ffn(1)
        for n in range(8):
            g, b = divmod(n, 2)
            act.wait_ge(out_turned, n + 1)
            fn(out_tok[:, b, g * 512:(g + 1) * 512], X[n % 4][:], ACT.Copy).then_inc(out_copied, 1)

    @block.gpsimd
    def _(pool):
        load_params(pool, 2)
        pool.memset(gate_w[:], 0.0).then_inc(gatew_zeroed, 1)
        pool.wait_ge(gatew_zeroed, 1)

        def gate_weights(i):
            for n, name in enumerate(("lru_gate_a_w", "lru_gate_x_w")):
                for e in range(2):
                    src = A[name][0].rearrange("(m e) a b -> a m e b", e=2)[:, ds(i * 2, 2), e, :]
                    pool.dma_start(gate_w[64 * e:64 * e + 64, 2 * n:2 * n + 2, 64 * e:64 * e + 64],
                                   src).then_inc(gatew_landed, 16)

        def sum_h_squares(t):
            c, t0 = (KT - 1) * t, FROM_IN[t]
            pool.wait_ge(h_squared, KT * t + 2)
            if t > 0:
                pool.wait_ge(pre_root, t)
            pool.tensor_tensor(h_sum[:, t0:T], mo[:, 0, t0:T], mo[:, 1, t0:T], ALU.add).then_inc(h_added, 1)
            with pool.Fori(2, KT) as m:
                pool.wait_ge(h_squared, m + (KT * t + 1))
                pool.wait_ge(h_added, m + (c - 1))
                pool.tensor_tensor(h_sum[:, t0:T], h_sum[:, t0:T], mo[:, m, t0:T], ALU.add).then_inc(h_added, 1)

        gate_weights(0)
        sum_h_squares(0)

        def a_squared(i):
            pool.wait_ge(decays_made, i + 1)
            pool.tensor_tensor(rg[:], aa[:], aa[:], ALU.mult).then_inc(a2_made, 1)

        with pool.Fori(0, 3) as i:
            pool.wait_ge(gates_summed, i + 1)
            gate_weights(i + 1)
            a_squared(i)
        a_squared(3)
        rwkv_pool(pool)

        def sum_squares(t):
            t0 = FROM_OUT[t]
            pool.memset(acc[:], 0.0).then_inc(added, 4)

            def body(i):
                for p in range(2):
                    pool.wait_ge(squared, i * 2 + (8 * t + p + 1))
                    for m in range(2):
                        c = 20 * t + 2 * p + m + 4
                        pool.wait_ge(added, i * 4 + c)
                        pool.tensor_tensor(acc[:, t0:T], acc[:, t0:T], sq[:, p, m, t0:T], ALU.add).then_inc(added, 1)
            with pool.Fori(0, 4) as i:
                body(i)

        pool.wait_ge(y_lo_made, Y_COUNT["out0"])
        sum_squares(0)
        if upto >= 2:
            sum_h_squares(1)
            pool.wait_ge(unit_used, UNITS * FIRST["dn0_2"])
            sum_squares(1)
        if upto >= 3:
            sum_h_squares(2)
            gla_pool(pool)
            pool.wait_ge(y_lo_made, Y_COUNT["out1"])
            sum_squares(2)
        if upto >= 4:
            sum_h_squares(3)
            pool.wait_ge(unit_used, UNITS * FIRST["dn1_2"])
            sum_squares(3)

    @block.vector
    def _(dve):
        link = Chain(dve, dve_chain)
        tt, stt, ts = nc.vector.tensor_tensor, nc.vector.scalar_tensor_tensor, nc.vector.tensor_scalar

        def stream(name, drain, steps=0, step=None):
            iters, panels = PLAN[name]

            def body(i):
                for p in range(len(panels)):
                    split_ahead(make_lo, dve, name, p, i, step)
                    if name in FRESH and isinstance(i, int) and i == 0 and p == 0:
                        dve.wait_ge(pre_root, FRESH[name] + 1)
                        t0 = FROM_IN[FRESH[name]]
                        link(nc.vector.reciprocal(rpre[:, t0:T], root[:, t0:T]))
                    drain(p, i)
            iterations(lambda start, stop: link.loop(stop - start, steps, start), name, body, name in FRESH)

        def scaled(dst, name, p, i):
            wait_panel(dve, name, p, i)
            n, t0 = FIRST[name] + p, first_token(name, p)
            tt(dst[:, :, t0:T], bank(n, t0), wide(rpre[:, t0:T]), ALU.mult).then_inc(drained[n % 2], 1)
            wait_drained(dve, name, p, i)

        def split_y(tiles, source, count, t0=0):
            dve.wait_ge(y_hi_made, count)
            tt(y_lo[:, tiles, t0:T], source, y_hi[:, tiles, t0:T].bitcast(F32), ALU.subtract).then_inc(y_lo_made, 1)

        def transition(t):
            t_out, t_in = FROM_OUT[t - 1], FROM_IN[t]
            if t < upto:
                split_before_norm(make_lo, dve, t)
            if t > 0:
                dve.wait_ge(post_root, t)
                link(nc.vector.reciprocal(rpost[:, t_out:T], root[:, t_out:T]))

            def times_rms(q):
                tiles = mo[:, ds(q * 2, 2), t_out:T]
                tt(tiles, tiles, wide(rpost[:, t_out:T]), ALU.mult).then_inc(normed, 1)

            def residual(q):
                dve.wait_ge(normed, q + (KT // 2 * (t - 1) + 1))
                for m in (q * 2, q * 2 + 1):
                    tile = h[:, ds(m, 1), t_out:T]
                    stt(tile, mo[:, ds(m, 1), t_out:T], post_w(t - 1, m), tile, ALU.mult, ALU.add).then_inc(h_ready, 1)

            def low(q):
                for e in range(2):
                    m = ds(q * 2 + e, 1)
                    dve.wait_ge(x_hi_made, q * 2 + (KT * t + 1 + e))
                    stt(x_lo[:, m, t_in:T], h[:, m, t_in:T], pre_w(t, q * 2 + e), x_hi[:, m, t_in:T].bitcast(F32),
                        ALU.mult, ALU.subtract).then_inc(x_lo_made, 1)
            pairs = KT // 2
            if t == 0:
                with dve.Fori(0, pairs) as q:
                    low(q)
                return
            times_rms(0)
            times_rms(1)
            residual(0)
            with dve.Fori(1, pairs - 1) as q:
                times_rms(q + 1)
                residual(q)
                if t < upto:
                    low(q - 1)
            residual(pairs - 1)
            if t < upto:
                low(pairs - 2)
                low(pairs - 1)

        nc.vector.memset(eps_col, NORM_EPS)
        nc.vector.memset(gn_eps_col, GN_EPS)
        dve.wait_ge(par_turned, 1)
        nc.vector.tensor_copy(params[:, 0:512], X[0][:])
        nc.vector.tensor_copy(params[:, 512:N_COLS], X[1][:, 0:N_COLS - 512]).then_inc(params_ready, 1)
        dve.wait_ge(params_ready, 1)
        link(ts(der("one_minus_mu", 0, 26), par("mu", 0, 26), -1.0, 1.0, ALU.mult, ALU.add))
        link(ts(der("one_minus_ka", 0, 8), par("k_a", 0, 8), -1.0, 1.0, ALU.mult, ALU.add))
        split_first(make_lo, dve, "wag")
        transition(0)

        def shifted(name, dst, mu_of):
            def drain(p, i):
                if name == "wag":
                    link(nc.vector.memset(u_in[:, :, 0:1], 0.0))
                scaled(u_in[:, :, 1:T + 1], name, p, i)
                for m in range(2):
                    link(ts(dst(p, i, m), u_in[:, m, 1:T + 1], der("one_minus_mu", mu_of(p, i, m)), None, ALU.mult))
                    link(stt(dst(p, i, m), u_in[:, m, 0:T], par("mu", mu_of(p, i, m)), dst(p, i, m), ALU.mult, ALU.add))
            return drain

        stream("wag", shifted("wag", lambda p, i, m: lora[:, m, :], lambda p, i, m: 24 + m))
        dve.sem_inc(lora_in, 1)
        dve.wait_ge(lam_exp, 1)
        x_c, z_c, z2_c, s_c, den_c = (small[:, T + 8 * k:T + 8 * k + 8] for k in range(5))
        link(ts(den_c, derived[:, 42:50], 2.0, None, ALU.add))
        link(nc.vector.reciprocal(den_c, den_c))
        link(tt(z_c, derived[:, 42:50], den_c, ALU.mult))
        link(tt(z2_c, z_c, z_c, ALU.mult))
        link(ts(s_c, z2_c, 1.0 / 15, None, ALU.mult))
        for k in (13, 11, 9, 7, 5, 3):
            link(stt(s_c, s_c, 1.0 / k, z2_c, ALU.add, ALU.mult))
        link(stt(s_c, s_c, 1.0, z_c, ALU.add, ALU.mult))
        link(ts(x_c, par("lam", 0, 8), -1.0, 0.0, ALU.mult, ALU.max))
        link(stt(s_c, s_c, 2.0, x_c, ALU.mult, ALU.add))
        link(ts(der("neg8sp", 0, 8), s_c, -8.0, None, ALU.mult))
        link(ts(der("pos8sp", 0, 8), s_c, 8.0, None, ALU.mult))
        stream("rkv", shifted("rkv", lambda p, i, m: rkv[:, i * 4 + (2 * p + m), :], lambda p, i, m: i * 4 + (2 * p + m)), 8)
        link(nc.vector.memset(lx_in[:, :, 0:3], 0.0))

        def lru(p, i):
            if p == 0:
                scaled(lx_in[:, :, 3:T + 3], "lru", 0, i)
                for m in range(2):
                    def tap(k):
                        return par("lru_cw", i * 2 + (8 * k + m))
                    link(ts(lx[:, m, :], lx_in[:, m, 3:T + 3], tap(3), par("lru_cb", i * 2 + m), ALU.mult, ALU.add))
                    for k in (2, 1, 0):
                        last = stt(lx[:, m, :], lx_in[:, m, k:k + T], tap(k), lx[:, m, :], ALU.mult, ALU.add)
                        if k or not m:
                            link(last)
                last.then_inc(lx_made, 1)
                return
            scaled(ly[:], "lru", 1, i)
            dve.wait_ge(lru_root, i + 1)
            link(tt(ig[:], ig[:], th[:], ALU.mult))
            for m in range(2):
                link(nc.vector.tensor_tensor_scan(lx[:, m, :], aa[:, m, :], ig[:, m, :], 0.0, ALU.mult, ALU.add))
            dve.wait_ge(lru_gelu, i + 1)
            tt(lx[:], lx[:], ly[:], ALU.mult).then_inc(lru_made, 1)
            split_y(ds(i * 2, 2), lx[:], i + 1)

        def lru_step(slot, i):
            if slot == 7:
                dve.wait_ge(gates_made, i + 1)
                link(tt(ig[:], ig[:], lx[:], ALU.mult))
                dve.wait_ge(a2_made, i + 1)
                stt(th[:], rg[:], 1.0, th[:], ALU.add, ALU.mult).then_inc(lru_root_in, 1)

        stream("lru", lru, 11, lru_step)
        rwkv_dve(dve, link, tt, stt, ts, split_y)

        def nothing(p, i):
            pass

        stream("out0", nothing)
        transition(1)

        def ffn(layer):
            link(nc.vector.memset(gate_in[:, :, 0:2], 0.0))
            for n in range(3):
                name = f"gv{layer}_{n}"

                def gate_value(p, i, name=name, n=n):
                    c, t0 = GV_COUNT[name], first_token(name, 1)
                    if p == 0:
                        scaled(gate_in[:, :, 2:T + 2], name, 0, i)
                        for m in range(2):
                            f = 2 * FFN_PARTS[n][0] + m
                            out = conv[:, m, t0:T]

                            def tap(k):
                                return par("ffn_cw", i * 2 + (132 * layer + 44 * k + f))

                            def back(k):
                                return gate_in[:, m, t0 + 2 - k:T + 2 - k]
                            link(ts(out, back(0), tap(2), par("ffn_cb", i * 2 + (44 * layer + f)), ALU.mult, ALU.add))
                            link(stt(out, back(1), tap(1), out, ALU.mult, ALU.add))
                            last = stt(out, back(2), tap(0), out, ALU.mult, ALU.add)
                        last.then_inc(conv_made, 1)
                    else:
                        scaled(val[:], name, 1, i)
                        dve.wait_ge(gelu_made, i + (c + 1))
                        tt(prod[:, :, t0:T], val[:, :, t0:T], gelu[:, :, t0:T], ALU.mult).then_inc(prod_made, 1)
                        split_y(ds(i * 2, 2), prod[:, :, t0:T], i + (Y_BEFORE[name.replace("gv", "dn")] + 1), t0)

                stream(name, gate_value, 4)

                def add_up(p, i, name=f"dn{layer}_{n}"):
                    wait_panel(dve, name, p, i)
                    t0 = first_token(name)
                    tiles = mo[:, ds(i * 4 + 2 * p, 2), t0:T]
                    tt(tiles, bank(FIRST[name] + p, t0), tiles, ALU.add).then_inc(drained[(FIRST[name] + p) % 2], 1)

                stream(f"dn{layer}_{n}", (nothing, add_up, add_up)[n])
            transition(2 * layer + 2)

        if upto >= 2:
            ffn(0)
        if upto >= 3:

            def q_or_k(p, i):
                scaled(qk[:, ds(i * 4 + 2 * p, 2), :], "gla_qk", p, i)
                if isinstance(i, int) and p == 1:
                    dve.wait_ge(gdw_landed, 16)
                    gd_pre = par("mix_pre", KT, KT).unsqueeze(2).broadcast_to([P, KT, 16])
                    tt(gd_w[:], gd_w[:], gd_pre, ALU.mult).then_inc(gdw_made, 1)
            stream("gla_qk", q_or_k)
            head_step, head_end = gla_dve(dve, link, tt, stt, ts, scaled)
            stream("gla_vg", head_end, GLA_STEPS, head_step)
            for m in range(0, KT, 2):
                split_y(slice(m, m + 2), o_gated[:, m:m + 2, :], Y_BEFORE["out1"] + m // 2 + 1)
            stream("out1", nothing)
            transition(3)
        if upto >= 4:
            ffn(1)


def flat_rows(ap):
    if len(ap.shape) == 2:
        return ap.rearrange("a (r p) -> (a r) p", p=P)
    if ap.shape[-1] == 64:
        return ap.rearrange("a (r e) c -> (a r) (e c)", e=2)
    return ap.rearrange("a k (r p) -> (a k r) p", p=P)


PARAM_SOURCE = {"mix_pre": "mix_pre_norm", "mix_post": "mix_post_norm", "ffn_pre": "ffn_pre_norm", "ffn_post": "ffn_post_norm",
                "lru_cw": "lru_conv_w", "lru_cb": "lru_conv_b", "ga_b": "lru_gate_a_b", "gx_b": "lru_gate_x_b",
                "lam": "lru_lambda", "mu": "rwkv_shift_mu", "w0": "rwkv_w0", "a0": "rwkv_a0", "k_k": "rwkv_k_k",
                "k_a": "rwkv_k_a", "r_k": "rwkv_r_k", "ln_w": "rwkv_ln_w", "ln_b": "rwkv_ln_b", "gk_b": "gla_gk_b",
                "gla_nw": "gla_norm_w", "ffn_cw": "ffn_conv_w", "ffn_cb": "ffn_conv_b"}


def param_spans():
    for name, rows in PARAM_ROWS:
        done = 0
        while done < rows:
            group, row = divmod(COL[name] + done, P)
            count = min(rows - done, P - row)
            yield name, done, group, row, count
            done += count


N_PARAM_DMAS = len(list(param_spans()))


def param_pieces(A):
    for name, done, group, row, count in param_spans():
        yield flat_rows(A[PARAM_SOURCE[name]])[done:done + count, :], group, row, count


_INS = ['x', 'meta_tokens', 'mix_pre_norm', 'mix_post_norm', 'ffn_pre_norm', 'ffn_post_norm', 'ab_w_in', 'lru_conv_w',
        'lru_conv_b', 'lru_gate_a_w', 'lru_gate_a_b', 'lru_gate_x_w', 'lru_gate_x_b', 'lru_lambda', 'rwkv_shift_mu',
        'rwkv_w0', 'rwkv_w2', 'rwkv_a0', 'rwkv_a2', 'rwkv_g2', 'rwkv_k_k', 'rwkv_k_a', 'rwkv_r_k', 'rwkv_ln_w',
        'rwkv_ln_b', 'ab_w_out', 'gla_w_in', 'gla_gk_up', 'gla_gk_b', 'gla_norm_w', 'gla_w_out', 'ffn_w_gate',
        'ffn_w_val', 'ffn_conv_w', 'ffn_conv_b', 'ffn_w_down']


def kernel(**inputs):
    import concourse.bacc as bacc
    from concourse.bass_utils import run_bass_kernel_spmd

    nc = bacc.Bacc("TRN2", target_bir_lowering=False, num_devices=1)
    arrays = {name: np.ascontiguousarray(inputs[name]) for name in _INS}
    arrays.update(zip(("const_rwkv", "const_gla", "const_trunk"), constants()))
    A = {name: nc.dram_tensor(name, a.shape, mybir.dt.from_np(a.dtype), kind="ExternalInput").ap()
         for name, a in arrays.items()}
    A["out"] = nc.dram_tensor("out", (1, SEQ, D_MODEL), F32, kind="ExternalOutput").ap()
    trunk_kernel(nc, A)
    r = run_bass_kernel_spmd(nc, [arrays], core_ids=[0])
    return r.results[0]["out"]
```
